# Optimizing a Trainium2 kernel written in Bass

```python
import jax, jax.numpy as jnp
from jax import lax
import numpy as np
import jax
import jax.numpy as jnp

D_MODEL = 1024
BATCH = 1
SEQ = 256
DEPTH = 2

GRID_W = 64
HEAD_DIM = 64
A_HEADS = 8
A_KV_HEADS = 2
B_HEADS = 8
B_KV_HEADS = 2
C_HEADS = D_MODEL // HEAD_DIM
Q_BLOCK = 128
WINDOW = 128
NA_KH = 8
NA_KW = 16
MEM_TOKENS = 256
MEM_HEADS = 4
MEM_HEAD_DIM = D_MODEL // MEM_HEADS
D_FF = 256 * ((8 * D_MODEL // 3 + 255) // 256)
ROPE_THETA = 10000.0
LN_EPS = 1e-5
RMS_EPS = 1e-6
ALPHA = (2.0 * DEPTH) ** 0.25
BETA = (8.0 * DEPTH) ** -0.25
N_EVEN = (DEPTH + 1) // 2
N_ODD = DEPTH // 2

A_Q = A_HEADS * HEAD_DIM
A_KV = A_KV_HEADS * HEAD_DIM
B_Q = B_HEADS * HEAD_DIM
B_KV = B_KV_HEADS * HEAD_DIM
AB_IN = A_Q + 2 * A_KV + B_Q + 2 * B_KV
AB_OUT = (A_HEADS + B_HEADS) * HEAD_DIM
AB_SPLITS = [A_Q, A_Q + A_KV, A_Q + 2 * A_KV, A_Q + 2 * A_KV + B_Q, A_Q + 2 * A_KV + B_Q + B_KV]
C_WIDTH = C_HEADS * HEAD_DIM


def layer_norm(x, g, b):
    xf = x.astype(jnp.float32)
    mu = xf.mean(-1, keepdims=True)
    var = jnp.square(xf - mu).mean(-1, keepdims=True)
    return ((xf - mu) * lax.rsqrt(var + LN_EPS) * g.astype(jnp.float32) + b.astype(jnp.float32)).astype(x.dtype)

def rms_norm(x, g):
    xf = x.astype(jnp.float32)
    return (xf * lax.rsqrt(jnp.mean(xf * xf, -1, keepdims=True) + RMS_EPS) * g.astype(jnp.float32)).astype(x.dtype)

def swiglu(x, w_gate, w_up, w_down):
    return (jax.nn.silu(x @ w_gate) * (x @ w_up)) @ w_down

def rope_angles(pos, dim):
    inv = ROPE_THETA ** (-jnp.arange(0, dim, 2, dtype=jnp.float32) / dim)
    return pos[:, None] * inv[None, :]

def apply_rope(x, ang):
    half = x.shape[-1] // 2
    cos = jnp.cos(ang)[None, :, None, :].astype(x.dtype)
    sin = jnp.sin(ang)[None, :, None, :].astype(x.dtype)
    x1, x2 = x[..., :half], x[..., half:]
    return jnp.concatenate([x1 * cos - x2 * sin, x2 * cos + x1 * sin], axis=-1)

def global_gqa(q, k, v):
    B, S, H, d = q.shape
    Hkv = k.shape[2]
    G = H // Hkv
    nb = S // Q_BLOCK
    scale = d ** -0.5
    qb = q.reshape(B, nb, Q_BLOCK, Hkv, G, d).transpose(1, 0, 2, 3, 4, 5)

    def one_block(q_blk):
        s = jnp.einsum('bqkgd,bskd->bkgqs', q_blk, k).astype(jnp.float32) * scale
        p = jax.nn.softmax(s, axis=-1).astype(v.dtype)
        return jnp.einsum('bkgqs,bskd->bqkgd', p, v)

    o = lax.map(one_block, qb)
    return o.transpose(1, 0, 2, 3, 4, 5).reshape(B, S, H * d)

def window_gqa_sink(q, k, v, sink):
    B, S, H, d = q.shape
    Hkv = k.shape[2]
    G = H // Hkv
    nb = S // Q_BLOCK
    scale = d ** -0.5
    qb = q.reshape(B, nb, Q_BLOCK, Hkv, G, d)
    pad = ((0, 0), (Q_BLOCK, Q_BLOCK), (0, 0), (0, 0))
    kp = jnp.pad(k, pad).reshape(B, nb + 2, Q_BLOCK, Hkv, d)
    vp = jnp.pad(v, pad).reshape(B, nb + 2, Q_BLOCK, Hkv, d)
    k_band = jnp.concatenate([kp[:, :-2], kp[:, 1:-1], kp[:, 2:]], axis=2)
    v_band = jnp.concatenate([vp[:, :-2], vp[:, 1:-1], vp[:, 2:]], axis=2)
    blk = jnp.arange(nb)[:, None] * Q_BLOCK
    qi = blk + jnp.arange(Q_BLOCK)[None, :]
    kj = blk - Q_BLOCK + jnp.arange(3 * Q_BLOCK)[None, :]
    rel = kj[:, None, :] - qi[:, :, None]
    valid = (jnp.abs(rel) <= WINDOW) & (kj[:, None, :] >= 0) & (kj[:, None, :] < S)
    s = jnp.einsum('bnqkgd,bnskd->bnkgqs', qb, k_band).astype(jnp.float32) * scale
    s = jnp.where(valid[None, :, None, None], s, -jnp.inf)
    sink_l = sink.astype(jnp.float32).reshape(Hkv, G)[None, None, :, :, None, None]
    m = jnp.maximum(s.max(-1, keepdims=True), sink_l)
    p = jnp.exp(s - m)
    p = (p / (p.sum(-1, keepdims=True) + jnp.exp(sink_l - m))).astype(v.dtype)
    o = jnp.einsum('bnkgqs,bnskd->bnqkgd', p, v_band)
    return o.reshape(B, S, H * d)

def mixer_ab(h, w_in, w_out, q_gain, k_gain, sink, ang_2d, ang_1d):
    B, S, _ = h.shape
    qa, ka, va, qb, kb, vb = jnp.split(h @ w_in, AB_SPLITS, axis=-1)
    qa = qa.reshape(B, S, A_HEADS, HEAD_DIM)
    ka = ka.reshape(B, S, A_KV_HEADS, HEAD_DIM)
    va = va.reshape(B, S, A_KV_HEADS, HEAD_DIM)
    qa = apply_rope(rms_norm(qa, q_gain), ang_2d)
    ka = apply_rope(rms_norm(ka, k_gain), ang_2d)
    out_a = global_gqa(qa, ka, va)
    qb = apply_rope(qb.reshape(B, S, B_HEADS, HEAD_DIM), ang_1d)
    kb = apply_rope(kb.reshape(B, S, B_KV_HEADS, HEAD_DIM), ang_1d)
    vb = vb.reshape(B, S, B_KV_HEADS, HEAD_DIM)
    out_b = window_gqa_sink(qb, kb, vb, sink)
    return jnp.concatenate([out_a, out_b], axis=-1) @ w_out

def mixer_c(h, w_in, w_out, rpb):
    B, S, _ = h.shape
    rows = S // GRID_W
    kh = min(NA_KH, rows)
    kw = NA_KW
    scale = HEAD_DIM ** -0.5
    q, k, v = jnp.split(h @ w_in, 3, axis=-1)
    qg = q.reshape(B, rows, GRID_W, C_HEADS, HEAD_DIM)
    kg = k.reshape(B, rows, GRID_W, C_HEADS, HEAD_DIM)
    vg = v.reshape(B, rows, GRID_W, C_HEADS, HEAD_DIM)
    col = jnp.arange(GRID_W)
    col_start = jnp.clip(col - kw // 2, 0, GRID_W - kw)
    col_idx = col_start[:, None] + jnp.arange(kw)[None, :]
    dc = col_idx - col[:, None]

    def row_block(r):
        rs = jnp.clip(r - kh // 2, 0, rows - kh)
        k_rows = lax.dynamic_slice_in_dim(kg, rs, kh, axis=1)
        v_rows = lax.dynamic_slice_in_dim(vg, rs, kh, axis=1)
        k_nb = jnp.take(k_rows, col_idx, axis=2)
        v_nb = jnp.take(v_rows, col_idx, axis=2)
        q_r = lax.dynamic_index_in_dim(qg, r, axis=1, keepdims=False)
        dr = rs + jnp.arange(kh) - r
        bias = rpb[:, dr[None, :, None] + NA_KH - 1, dc[:, None, :] + NA_KW - 1]
        s = jnp.einsum('bwhd,bawjhd->bhwaj', q_r, k_nb).astype(jnp.float32) * scale
        s = s + bias.astype(jnp.float32)[None]
        p = jax.nn.softmax(s.reshape(B, C_HEADS, GRID_W, kh * kw), axis=-1)
        p = p.reshape(B, C_HEADS, GRID_W, kh, kw).astype(v.dtype)
        return jnp.einsum('bhwaj,bawjhd->bwhd', p, v_nb)

    o = lax.map(row_block, jnp.arange(rows))
    o = o.transpose(1, 0, 2, 3, 4).reshape(B, S, C_WIDTH)
    return o @ w_out

def memory_attn(h, mem, w_q, w_kv, w_o):
    B, S, _ = h.shape
    M = mem.shape[1]
    q = (h @ w_q).reshape(B, S, MEM_HEADS, MEM_HEAD_DIM)
    k, v = jnp.split(mem @ w_kv, 2, axis=-1)
    k = k.reshape(B, M, MEM_HEADS, MEM_HEAD_DIM)
    v = v.reshape(B, M, MEM_HEADS, MEM_HEAD_DIM)
    s = jnp.einsum('bshd,bmhd->bhsm', q, k).astype(jnp.float32) * (MEM_HEAD_DIM ** -0.5)
    p = jax.nn.softmax(s, axis=-1).astype(v.dtype)
    o = jnp.einsum('bhsm,bmhd->bshd', p, v).reshape(B, S, D_MODEL)
    return o @ w_o

def first_inputs(seed: int = 0) -> dict:
    key = jax.random.key(seed)
    ks = jax.random.split(key, 20)
    nrm = jax.random.normal
    f32 = jnp.float32
    d_sc = D_MODEL ** -0.5
    return {
        "x": nrm(ks[0], (BATCH, SEQ, D_MODEL), f32),
        "mem": nrm(ks[1], (BATCH, MEM_TOKENS, D_MODEL), f32),
        "ln_g": 1.0 + 0.02 * nrm(ks[2], (DEPTH, 4, D_MODEL), f32),
        "ln_b": 0.02 * nrm(ks[3], (DEPTH, 4, D_MODEL), f32),
        "ffn_w_gate": nrm(ks[4], (DEPTH, 2, D_MODEL, D_FF), f32) * d_sc,
        "ffn_w_up": nrm(ks[5], (DEPTH, 2, D_MODEL, D_FF), f32) * d_sc,
        "ffn_w_down": nrm(ks[6], (DEPTH, 2, D_FF, D_MODEL), f32) * (D_FF ** -0.5) * BETA,
        "ab_w_in": nrm(ks[7], (N_EVEN, D_MODEL, AB_IN), f32) * d_sc,
        "ab_w_out": nrm(ks[8], (N_EVEN, AB_OUT, D_MODEL), f32) * (AB_OUT ** -0.5) * BETA,
        "ab_q_gain": 1.0 + 0.02 * nrm(ks[9], (N_EVEN, HEAD_DIM), f32),
        "ab_k_gain": 1.0 + 0.02 * nrm(ks[10], (N_EVEN, HEAD_DIM), f32),
        "ab_sink": 0.5 * nrm(ks[11], (N_EVEN, B_HEADS), f32),
        "c_w_in": nrm(ks[12], (N_ODD, D_MODEL, 3 * C_WIDTH), f32) * d_sc,
        "c_w_out": nrm(ks[13], (N_ODD, C_WIDTH, D_MODEL), f32) * (C_WIDTH ** -0.5) * BETA,
        "c_rpb": 0.1 * nrm(ks[14], (N_ODD, C_HEADS, 2 * NA_KH - 1, 2 * NA_KW - 1), f32),
        "mem_w_q": nrm(ks[15], (DEPTH, D_MODEL, D_MODEL), f32) * d_sc,
        "mem_w_kv": nrm(ks[16], (DEPTH, D_MODEL, 2 * D_MODEL), f32) * d_sc,
        "mem_w_o": nrm(ks[17], (DEPTH, D_MODEL, D_MODEL), f32) * d_sc * BETA,
    }

def first_block(x, mem, ln_g, ln_b, ffn_w_gate, ffn_w_up, ffn_w_down,
              ab_w_in, ab_w_out, ab_q_gain, ab_k_gain, ab_sink,
              c_w_in, c_w_out, c_rpb, mem_w_q, mem_w_kv, mem_w_o):
    S = x.shape[1]
    t = jnp.arange(S)
    row = (t // GRID_W).astype(jnp.float32)
    colp = (t % GRID_W).astype(jnp.float32)
    ang_2d = jnp.concatenate([rope_angles(row, HEAD_DIM // 2), rope_angles(colp, HEAD_DIM // 2)], axis=-1)
    ang_1d = rope_angles(t.astype(jnp.float32), HEAD_DIM)
    for i in range(DEPTH):
        j = i // 2
        y = swiglu(x, ffn_w_gate[i, 0], ffn_w_up[i, 0], ffn_w_down[i, 0])
        x = layer_norm(ALPHA * x + 0.5 * y, ln_g[i, 0], ln_b[i, 0])
        if i % 2 == 0:
            y = mixer_ab(x, ab_w_in[j], ab_w_out[j], ab_q_gain[j], ab_k_gain[j], ab_sink[j], ang_2d, ang_1d)
        else:
            y = mixer_c(x, c_w_in[j], c_w_out[j], c_rpb[j])
        x = layer_norm(ALPHA * x + y, ln_g[i, 1], ln_b[i, 1])
        y = memory_attn(x, mem, mem_w_q[i], mem_w_kv[i], mem_w_o[i])
        x = layer_norm(ALPHA * x + y, ln_g[i, 2], ln_b[i, 2])
        y = swiglu(x, ffn_w_gate[i, 1], ffn_w_up[i, 1], ffn_w_down[i, 1])
        x = layer_norm(ALPHA * x + 0.5 * y, ln_g[i, 3], ln_b[i, 3])
    return x


CHUNK = 64
N_MEM = 256
NORM_EPS = 1e-6
NEG_INF = -1e30

RWKV_HEADS = 8
RWKV_HEAD_DIM = 64
RWKV_DIM = RWKV_HEADS * RWKV_HEAD_DIM
RWKV_DECAY_RANK = 64
RWKV_A_RANK = 64
RWKV_V_RANK = 32
RWKV_GATE_RANK = 128
RWKV_LNX_EPS = 1e-5 * RWKV_HEAD_DIM
RWKV_SIZES = (RWKV_DIM, RWKV_DIM, RWKV_DIM, RWKV_DECAY_RANK, RWKV_A_RANK, RWKV_GATE_RANK)
RWKV_COLS = sum(RWKV_SIZES)

DSA_HEADS = 8
DSA_HEAD_DIM = 64
DSA_DIM = DSA_HEADS * DSA_HEAD_DIM
IDX_HEADS = 8
IDX_DIM = 64
DSA_TOPK_MAX = 256
DSA_SIZES = (DSA_DIM, DSA_HEAD_DIM, DSA_HEAD_DIM, IDX_HEADS * IDX_DIM, IDX_DIM, IDX_HEADS)
DSA_COLS = sum(DSA_SIZES)

IN_SIZES = (RWKV_COLS, DSA_COLS, D_MODEL, D_MODEL)
N_IN = sum(IN_SIZES)

MEM_HEAD_DIM_2 = 128
MEM_DIM = MEM_HEADS * MEM_HEAD_DIM_2

FFN_DIM = 2816
N_EXPERTS = 8
TOP_K = 2
EXPERT_DIM = 1408
N_DENSE = (DEPTH + 1) // 2
N_MOE = DEPTH // 2


def split_cols(t, sizes):
    return jnp.split(t, np.cumsum(sizes)[:-1].tolist(), axis=-1)

def rms_norm_2(x, g):
    x32 = x.astype(jnp.float32)
    y = x32 * lax.rsqrt(jnp.mean(x32 * x32, axis=-1, keepdims=True) + NORM_EPS)
    return (y * g.astype(jnp.float32)).astype(x.dtype)

def rope_tables(positions, dim):
    inv_freq = 1.0 / (ROPE_THETA ** (jnp.arange(0, dim, 2, dtype=jnp.float32) / dim))
    ang = positions.astype(jnp.float32)[..., None] * inv_freq
    return jnp.cos(ang), jnp.sin(ang)

def apply_rope_2(x, cos, sin):
    shape = cos.shape[:2] + (1,) * (x.ndim - 3) + cos.shape[2:]
    c, s = cos.reshape(shape), sin.reshape(shape)
    x1, x2 = jnp.split(x.astype(jnp.float32), 2, axis=-1)
    return jnp.concatenate([x1 * c - x2 * s, x2 * c + x1 * s], axis=-1).astype(x.dtype)

def token_shift(t):
    return jnp.pad(t[:, :-1], ((0, 0), (1, 0), (0, 0)))

def rwkv7_scan(r, w, k, v, a, b):
    bsz, _, h, n = r.shape
    xs = tuple(jnp.moveaxis(t, 1, 0) for t in (r, w, k, v, a, b))

    def step(state, inp):
        r_t, w_t, k_t, v_t, a_t, b_t = inp
        sa = jnp.einsum('bhvk,bhk->bhv', state, a_t)
        state = (state * w_t[:, :, None, :] + sa[..., None] * b_t[:, :, None, :]
                 + v_t[..., None] * k_t[:, :, None, :])
        return state, jnp.einsum('bhvk,bhk->bhv', state, r_t)

    _, ys = lax.scan(step, jnp.zeros((bsz, h, n, n), jnp.float32), xs)
    return jnp.moveaxis(ys, 0, 1)

def rwkv7_branch(cols, v_first, mu, w0, w2, a0, a2, g2, v_mix, k_k, k_a, r_k, lnx_g, lnx_b):
    bsz, seqlen, _ = cols.shape
    cols = cols + (token_shift(cols) - cols) * mu
    r, k, v, wd, ad, gd = split_cols(cols, RWKV_SIZES)
    w_log = -jax.nn.softplus(-(w0 + jnp.tanh(wd) @ w2)) - 0.5
    a = jax.nn.sigmoid(a0 + ad @ a2)
    g = jax.nn.sigmoid(gd) @ g2
    if v_mix is None:
        v_first = v
    else:
        v0, v1, v2 = v_mix
        v = v + (v_first - v) * jax.nn.sigmoid(v0 + (v @ v1) @ v2)
    heads = lambda t: t.astype(jnp.float32).reshape(bsz, seqlen, RWKV_HEADS, RWKV_HEAD_DIM)
    kk = heads(k * k_k)
    kk = kk / jnp.maximum(jnp.sqrt(jnp.sum(kk * kk, axis=-1, keepdims=True)), 1e-12)
    k = k * (1.0 + (a - 1.0) * k_a)
    rh, kh, vh, ah = heads(r), heads(k), heads(v), heads(a)
    decay = jnp.exp(-jnp.exp(heads(w_log)))
    y = rwkv7_scan(rh, decay, kh, vh, -kk, kk * ah)
    mean = jnp.mean(y, axis=-1, keepdims=True)
    var = jnp.mean(jnp.square(y - mean), axis=-1, keepdims=True)
    y = (y - mean) * lax.rsqrt(var + RWKV_LNX_EPS)
    y = y.reshape(bsz, seqlen, RWKV_DIM) * lnx_g.astype(jnp.float32) + lnx_b.astype(jnp.float32)
    bonus = jnp.sum(rh * kh * r_k.astype(jnp.float32), axis=-1, keepdims=True) * vh
    y = y + bonus.reshape(bsz, seqlen, RWKV_DIM)
    return (y * g.astype(jnp.float32)).astype(cols.dtype), v_first

def dsa_attention(q, k, v, q_idx, k_idx, w_idx):
    length = q.shape[1]
    top_k = min(DSA_TOPK_MAX, length // 4)
    key_pos = jnp.arange(length)
    gather = jax.vmap(lambda t, i: t[i])
    k_idx32 = k_idx.astype(jnp.float32)

    def query_block(i):
        start = i * Q_BLOCK
        qb = lax.dynamic_slice_in_dim(q, start, Q_BLOCK, axis=1)
        qib = lax.dynamic_slice_in_dim(q_idx, start, Q_BLOCK, axis=1).astype(jnp.float32)
        wb = lax.dynamic_slice_in_dim(w_idx, start, Q_BLOCK, axis=1).astype(jnp.float32)
        limit = ((start + jnp.arange(Q_BLOCK)) // CHUNK + 1) * CHUNK
        admissible = key_pos[None, :] < limit[:, None]
        logits = jnp.einsum('bqhd,bsd->bqhs', qib, k_idx32) * (IDX_DIM ** -0.5)
        score = jnp.einsum('bqhs,bqh->bqs', jax.nn.relu(logits), wb) * (IDX_HEADS ** -0.5)
        score = jnp.where(admissible[None], score, NEG_INF)
        _, sel = lax.top_k(score, top_k)
        valid = sel < limit[None, :, None]
        ks, vs = gather(k, sel), gather(v, sel)
        s = jnp.einsum('bqhd,bqkd->bqhk', qb, ks).astype(jnp.float32) * (DSA_HEAD_DIM ** -0.5)
        p = jax.nn.softmax(jnp.where(valid[:, :, None, :], s, NEG_INF), axis=-1)
        return jnp.einsum('bqhk,bqkd->bqhd', p.astype(vs.dtype), vs)

    out = lax.map(query_block, jnp.arange(length // Q_BLOCK))
    return jnp.moveaxis(out, 0, 1).reshape(q.shape)

def dsa_branch(cols, cos_q, sin_q, cos_i, sin_i, q_norm, k_norm, idx_k_norm):
    bsz, seqlen, _ = cols.shape
    q, k, v, iq, ik, iw = split_cols(cols, DSA_SIZES)
    q = apply_rope_2(rms_norm_2(q.reshape(bsz, seqlen, DSA_HEADS, DSA_HEAD_DIM), q_norm), cos_q, sin_q)
    k = apply_rope_2(rms_norm_2(k, k_norm), cos_q, sin_q)
    iq = apply_rope_2(iq.reshape(bsz, seqlen, IDX_HEADS, IDX_DIM), cos_i, sin_i)
    ik = apply_rope_2(rms_norm_2(ik, idx_k_norm), cos_i, sin_i)
    return dsa_attention(q, k, v, iq, ik, iw).reshape(bsz, seqlen, DSA_DIM)

def memory_attention(h, mem_n, wq, wkv, q_norm, k_norm, wo):
    bsz, seqlen, _ = h.shape
    n_mem = mem_n.shape[1]
    q = rms_norm_2((h @ wq).reshape(bsz, seqlen, MEM_HEADS, MEM_HEAD_DIM_2), q_norm)
    k, v = split_cols(mem_n @ wkv, (MEM_DIM, MEM_DIM))
    k = rms_norm_2(k.reshape(bsz, n_mem, MEM_HEADS, MEM_HEAD_DIM_2), k_norm)
    v = v.reshape(bsz, n_mem, MEM_HEADS, MEM_HEAD_DIM_2)
    s = jnp.einsum('bshd,bmhd->bhsm', q, k).astype(jnp.float32) * (MEM_HEAD_DIM_2 ** -0.5)
    p = jax.nn.softmax(s, axis=-1).astype(v.dtype)
    o = jnp.einsum('bhsm,bmhd->bshd', p, v).reshape(bsz, seqlen, MEM_DIM)
    return o @ wo

def swiglu_2(h, wg, wu, wd):
    return (jax.nn.silu(h @ wg) * (h @ wu)) @ wd

def moe_swiglu(h, router, bias, wg, wu, wd):
    logits = (h @ router).astype(jnp.float32) + bias.astype(jnp.float32)
    top_logit, top_idx = lax.top_k(logits, TOP_K)
    top_w = jax.nn.softmax(top_logit, axis=-1)
    gates = jnp.sum(jax.nn.one_hot(top_idx, N_EXPERTS, dtype=jnp.float32) * top_w[..., None], axis=-2)
    gates = gates.astype(h.dtype)
    out = jnp.zeros_like(h)
    for e in range(N_EXPERTS):
        out = out + gates[..., e:e + 1] * swiglu_2(h, wg[e], wu[e], wd[e])
    return out

def second_inputs(seed: int = 0) -> dict:
    keys = iter(jax.random.split(jax.random.key(seed), 48))
    f32 = jnp.float32

    def normal(shape, scale):
        return jax.random.normal(next(keys), shape, f32) * scale

    def gain(shape):
        return 1.0 + normal(shape, 0.02)

    x = normal((BATCH, SEQ, D_MODEL), 1.0)
    mem = normal((BATCH, N_MEM, D_MODEL), 1.0)
    offsets = jax.random.randint(next(keys), (BATCH, 1), 0, 64) * CHUNK
    positions = (offsets + jnp.arange(SEQ)[None, :]).astype(jnp.int32)
    nv = DEPTH - 1
    return {
        'x': x,
        'mem': mem,
        'positions': positions,
        'norm_mix': gain((DEPTH, D_MODEL)),
        'w_in': normal((DEPTH, D_MODEL, N_IN), D_MODEL ** -0.5),
        'rwkv_mu': jax.random.uniform(next(keys), (DEPTH, RWKV_COLS), f32, 0.0, 1.0),
        'rwkv_w0': jax.random.uniform(next(keys), (DEPTH, RWKV_DIM), f32, -6.0, -1.0),
        'rwkv_w2': normal((DEPTH, RWKV_DECAY_RANK, RWKV_DIM), 0.5 * RWKV_DECAY_RANK ** -0.5),
        'rwkv_a0': normal((DEPTH, RWKV_DIM), 0.1),
        'rwkv_a2': normal((DEPTH, RWKV_A_RANK, RWKV_DIM), RWKV_A_RANK ** -0.5),
        'rwkv_g2': normal((DEPTH, RWKV_GATE_RANK, RWKV_DIM), RWKV_GATE_RANK ** -0.5),
        'rwkv_v0': normal((nv, RWKV_DIM), 0.5),
        'rwkv_v1': normal((nv, RWKV_DIM, RWKV_V_RANK), RWKV_DIM ** -0.5),
        'rwkv_v2': normal((nv, RWKV_V_RANK, RWKV_DIM), RWKV_V_RANK ** -0.5),
        'rwkv_kk': 0.85 + normal((DEPTH, RWKV_DIM), 0.02),
        'rwkv_ka': gain((DEPTH, RWKV_DIM)),
        'rwkv_rk': normal((DEPTH, RWKV_HEADS, RWKV_HEAD_DIM), 0.1),
        'rwkv_lnx_g': gain((DEPTH, RWKV_DIM)),
        'rwkv_lnx_b': normal((DEPTH, RWKV_DIM), 0.02),
        'dsa_q_norm': gain((DEPTH, DSA_HEAD_DIM)),
        'dsa_k_norm': gain((DEPTH, DSA_HEAD_DIM)),
        'idx_k_norm': gain((DEPTH, IDX_DIM)),
        'w_branch_a': normal((DEPTH, RWKV_DIM, D_MODEL), RWKV_DIM ** -0.5),
        'w_branch_b': normal((DEPTH, DSA_DIM, D_MODEL), DSA_DIM ** -0.5),
        'w_out': normal((DEPTH, D_MODEL, D_MODEL), 0.5 * D_MODEL ** -0.5),
        'norm_mem': gain((DEPTH, D_MODEL)),
        'mem_tok_norm': gain((DEPTH, D_MODEL)),
        'mem_wq': normal((DEPTH, D_MODEL, MEM_DIM), D_MODEL ** -0.5),
        'mem_wkv': normal((DEPTH, D_MODEL, 2 * MEM_DIM), D_MODEL ** -0.5),
        'mem_q_norm': gain((DEPTH, MEM_HEAD_DIM_2)),
        'mem_k_norm': gain((DEPTH, MEM_HEAD_DIM_2)),
        'mem_wo': normal((DEPTH, MEM_DIM, D_MODEL), 0.5 * MEM_DIM ** -0.5),
        'norm_ffn': gain((DEPTH, D_MODEL)),
        'ffn_wg': normal((N_DENSE, D_MODEL, FFN_DIM), D_MODEL ** -0.5),
        'ffn_wu': normal((N_DENSE, D_MODEL, FFN_DIM), D_MODEL ** -0.5),
        'ffn_wd': normal((N_DENSE, FFN_DIM, D_MODEL), 0.5 * FFN_DIM ** -0.5),
        'moe_router': normal((N_MOE, D_MODEL, N_EXPERTS), D_MODEL ** -0.5),
        'moe_bias': normal((N_MOE, N_EXPERTS), 0.01),
        'moe_wg': normal((N_MOE, N_EXPERTS, D_MODEL, EXPERT_DIM), D_MODEL ** -0.5),
        'moe_wu': normal((N_MOE, N_EXPERTS, D_MODEL, EXPERT_DIM), D_MODEL ** -0.5),
        'moe_wd': normal((N_MOE, N_EXPERTS, EXPERT_DIM, D_MODEL), 0.5 * EXPERT_DIM ** -0.5),
    }

def second_block(x, mem, positions, norm_mix, w_in, rwkv_mu, rwkv_w0, rwkv_w2, rwkv_a0, rwkv_a2,
              rwkv_g2, rwkv_v0, rwkv_v1, rwkv_v2, rwkv_kk, rwkv_ka, rwkv_rk, rwkv_lnx_g, rwkv_lnx_b,
              dsa_q_norm, dsa_k_norm, idx_k_norm, w_branch_a, w_branch_b, w_out, norm_mem,
              mem_tok_norm, mem_wq, mem_wkv, mem_q_norm, mem_k_norm, mem_wo, norm_ffn, ffn_wg,
              ffn_wu, ffn_wd, moe_router, moe_bias, moe_wg, moe_wu, moe_wd):
    cos_q, sin_q = rope_tables(positions, DSA_HEAD_DIM)
    cos_i, sin_i = rope_tables(positions, IDX_DIM)
    v_first = None
    for l in range(DEPTH):
        h = rms_norm_2(x, norm_mix[l])
        cols_a, cols_b, gate_a, gate_b = split_cols(h @ w_in[l], IN_SIZES)
        v_mix = None if l == 0 else (rwkv_v0[l - 1], rwkv_v1[l - 1], rwkv_v2[l - 1])
        y_a, v_first = rwkv7_branch(cols_a, v_first, rwkv_mu[l], rwkv_w0[l], rwkv_w2[l], rwkv_a0[l],
                                    rwkv_a2[l], rwkv_g2[l], v_mix, rwkv_kk[l], rwkv_ka[l], rwkv_rk[l],
                                    rwkv_lnx_g[l], rwkv_lnx_b[l])
        y_b = dsa_branch(cols_b, cos_q, sin_q, cos_i, sin_i, dsa_q_norm[l], dsa_k_norm[l], idx_k_norm[l])
        merged = (jax.nn.sigmoid(gate_a) * (y_a @ w_branch_a[l])
                  + jax.nn.sigmoid(gate_b) * (y_b @ w_branch_b[l]))
        x = x + merged @ w_out[l]
        x = x + memory_attention(rms_norm_2(x, norm_mem[l]), rms_norm_2(mem, mem_tok_norm[l]), mem_wq[l],
                                 mem_wkv[l], mem_q_norm[l], mem_k_norm[l], mem_wo[l])
        h = rms_norm_2(x, norm_ffn[l])
        j = l // 2
        if l % 2 == 0:
            x = x + swiglu_2(h, ffn_wg[j], ffn_wu[j], ffn_wd[j])
        else:
            x = x + moe_swiglu(h, moe_router[j], moe_bias[j], moe_wg[j], moe_wu[j], moe_wd[j])
    return x


def setup_inputs(seed=0):
    out = dict(first_inputs(seed))
    for name, value in second_inputs(seed + 1).items():
        if name != "x":
            out[name + "_2"] = value
    return out


def reference(
    x, mem, ln_g, ln_b, ffn_w_gate, ffn_w_up, ffn_w_down, ab_w_in, ab_w_out, ab_q_gain,
    ab_k_gain, ab_sink, c_w_in, c_w_out, c_rpb, mem_w_q, mem_w_kv, mem_w_o, mem_2, positions_2,
    norm_mix_2, w_in_2, rwkv_mu_2, rwkv_w0_2, rwkv_w2_2, rwkv_a0_2, rwkv_a2_2, rwkv_g2_2,
    rwkv_v0_2, rwkv_v1_2, rwkv_v2_2, rwkv_kk_2, rwkv_ka_2, rwkv_rk_2, rwkv_lnx_g_2,
    rwkv_lnx_b_2, dsa_q_norm_2, dsa_k_norm_2, idx_k_norm_2, w_branch_a_2, w_branch_b_2, w_out_2,
    norm_mem_2, mem_tok_norm_2, mem_wq_2, mem_wkv_2, mem_q_norm_2, mem_k_norm_2, mem_wo_2,
    norm_ffn_2, ffn_wg_2, ffn_wu_2, ffn_wd_2, moe_router_2, moe_bias_2, moe_wg_2, moe_wu_2,
    moe_wd_2,
):
    x = first_block(
        x, mem, ln_g, ln_b, ffn_w_gate, ffn_w_up, ffn_w_down, ab_w_in, ab_w_out, ab_q_gain,
        ab_k_gain, ab_sink, c_w_in, c_w_out, c_rpb, mem_w_q, mem_w_kv, mem_w_o,
    )
    return second_block(
        x, mem_2, positions_2, norm_mix_2, w_in_2, rwkv_mu_2, rwkv_w0_2, rwkv_w2_2, rwkv_a0_2,
        rwkv_a2_2, rwkv_g2_2, rwkv_v0_2, rwkv_v1_2, rwkv_v2_2, rwkv_kk_2, rwkv_ka_2, rwkv_rk_2,
        rwkv_lnx_g_2, rwkv_lnx_b_2, dsa_q_norm_2, dsa_k_norm_2, idx_k_norm_2, w_branch_a_2,
        w_branch_b_2, w_out_2, norm_mem_2, mem_tok_norm_2, mem_wq_2, mem_wkv_2, mem_q_norm_2,
        mem_k_norm_2, mem_wo_2, norm_ffn_2, ffn_wg_2, ffn_wu_2, ffn_wd_2, moe_router_2,
        moe_bias_2, moe_wg_2, moe_wu_2, moe_wd_2,
    )


_drawn_inputs = setup_inputs


def setup_inputs(seed=0):
    import zlib

    import numpy as np

    out = dict(_drawn_inputs(seed))
    spreads = {}
    factors = {'ab_q_gain': 7.694,
     'ab_k_gain': 5.534,
     'ab_sink': 8.0,
     'c_rpb': 3.261,
     'norm_mix_2': 2.866,
     'rwkv_w2_2': 4.41,
     'rwkv_a0_2': 3.54,
     'rwkv_kk_2': 6.409,
     'rwkv_ka_2': 6.532,
     'rwkv_lnx_g_2': 5.412,
     'rwkv_lnx_b_2': 4.722,
     'dsa_q_norm_2': 7.731,
     'dsa_k_norm_2': 8.0,
     'idx_k_norm_2': 3.225,
     'norm_mem_2': 7.583,
     'mem_tok_norm_2': 8.0,
     'mem_q_norm_2': 8.0,
     'mem_k_norm_2': 5.481,
     'moe_bias_2': 30.616,
     'norm_ffn_2': 3.753,
     'moe_router_2': 2.894,
     'moe_wg_2': 2.751}
    for name, (base, spread) in spreads.items():
        noise = np.random.default_rng([zlib.crc32(name.encode()), seed]).standard_normal(out[name].shape)
        drawn = base * np.exp(spread * noise) if base else spread * noise
        out[name] = jnp.asarray(drawn.astype(out[name].dtype))
    for name, factor in factors.items():
        out[name] = (out[name] * factor).astype(out[name].dtype)
    return out
```

```python
from contextlib import ExitStack

import numpy as np

import concourse.bass as bass
from concourse import mybir

F32 = mybir.dt.float32
F32R = mybir.dt.float32r
I32 = mybir.dt.int32
ALU = mybir.AluOpType
ACT = mybir.ActivationFunctionType
AX = mybir.AxisListType.X

P = 128
S = 256
MT = S // P
D = 1024
KT = D // P
D_FF = 2816
HD = 64
GRID_W = 64
ALPHA = (2.0 * 2) ** 0.25
LN_EPS = 1e-5
RMS_EPS = 1e-6
NEG = -1e30
BANK = 512
SLOT = 2048
SLOTS = 5
HIGH_SLOTS = 4
CH = 64
AREA = 21000
AREA_HALVES = 10240
N_EXPERTS = 8
EXPERT_DIM = 1408



class Ledger:

    def __init__(self, nc, ctx, known):
        self.nc, self.ctx, self.known = nc, ctx, known
        self.sems, self.total, self.counts = {}, {}, {}
        self.drains, self.group_number = [], {}

    def sem(self, topic):
        if topic not in self.sems:
            self.sems[topic] = self.ctx.enter_context(self.nc.semaphore(topic))
            self.total[topic] = 0
        return self.sems[topic]

    def count(self, topic, names, by):
        sem = self.sem(topic)
        self.total[topic] += by
        for name in names:
            assert name not in self.counts, name
            self.counts[name] = (topic, self.total[topic])
        return sem, by

    def values(self):
        for group, n in self.group_number.items():
            bank = self.counts[group][0][4]
            self.counts[("drained", group)] = (f"psum{bank}_empty", n)
        for events, bank, group in self.drains:
            for event in events:
                self.counts[event] = (f"psum{bank}_empty", self.group_number[group])
        return self.counts


class Engine:

    def __init__(self, ledger, raw, name):
        self.ledger, self.raw, self.name = ledger, raw, name
        self.seen = {}
        self.last = []

    def wait_ge(self, *counts):
        for topic, value in counts:
            if value > self.seen.get(topic, 0):
                self.raw.wait_ge(self.ledger.sem(topic), value)
                self.seen[topic] = value

    def at(self, *events):
        return [self.ledger.known[e] for e in events] if self.ledger.known is not None else []

    def mark(self, topic, *events, by=1):
        out = self.ledger.count(topic, events, by)
        self.last = [(topic, self.ledger.total[topic])]
        return out

    def step(self):
        return self.mark(self.name + "_step")



def _rope_tables():
    t = np.arange(S)
    inv = lambda dim: (np.float32(10000.0) ** (-np.arange(0, dim, 2, dtype=np.float32) / np.float32(dim))).astype(np.float32)
    row = (t // GRID_W).astype(np.float32)
    col = (t % GRID_W).astype(np.float32)
    a2 = np.concatenate([row[:, None] * inv(32)[None], col[:, None] * inv(32)[None]], -1).astype(np.float32)
    a1 = (t.astype(np.float32)[:, None] * inv(64)[None]).astype(np.float32)
    return a2, a1


def _constants():
    out = {}
    tok = lambda a: a.reshape(MT, P, -1).transpose(1, 0, 2).reshape(P, -1)
    out["ident"] = np.eye(P)
    a2, a1 = _rope_tables()
    out["cos2"], out["sin2"] = tok(np.cos(a2)), tok(np.sin(a2))
    out["cos1"], out["sin1"] = tok(np.cos(a1)), tok(np.sin(a1))
    q, k = np.arange(S)[:, None], np.arange(S)[None, :]
    out["window"] = tok(np.where(np.abs(q - k) <= 128, 0.0, NEG))
    start = np.clip(q % GRID_W - 8, 0, GRID_W - 16)
    out["columns"] = tok(np.where((k % GRID_W >= start) & (k % GRID_W < start + 16), 0.0, NEG))
    out["admissible"] = tok(np.where(k < (q // 64 + 1) * 64, 0.0, 1.0) * NEG)
    s, t = np.arange(P)[:, None], np.arange(P)[None, :]
    same = (s // CH) == (t // CH)
    strict, incl = same & (s < t), same & (s <= t)
    out["before"] = strict
    out["upto"] = incl
    for n in (1, 2, 4, 8, 16, 32):
        out[f"level{n}"] = (s // (2 * n) == t // (2 * n)) & (s // n % 2 == 1) & (t // n % 2 == 0)
    inv = 1.0 / (np.float32(10000.0) ** (np.arange(0, 64, 2, dtype=np.float32) / np.float32(64)))
    out["inv_freq"] = np.tile(inv.astype(np.float32)[None], (P, 1))
    t = np.arange(CH)[None, :]
    out["packed"] = np.concatenate([s % CH <= t, s % CH < t, s % CH <= t], axis=1)
    out["lower_index"] = np.tile((np.arange(8)[None, :] < np.arange(8)[:, None]).reshape(1, 64), (P, 1))
    out["minus_half"] = np.full((P, 32), -0.5)
    return {n: np.ascontiguousarray(a, dtype=np.float32) for n, a in out.items()}


CONSTANTS = _constants()
CONST_AT = {}
_at = 0
for _n, _a in CONSTANTS.items():
    CONST_AT[_n] = (_at, _a.shape[1])
    _at += _a.shape[1]
CONST_COLS = _at
CONST_ARRAY = np.ascontiguousarray(np.concatenate(list(CONSTANTS.values()), axis=1))


def row_tile(v, m):
    return slice(m * P, (m + 1) * P)


def pick(t, rows, m):
    if isinstance(t, tuple):
        return t[0][:, rows, m * P:(m + 1) * P], t[1][:, rows, m * P:(m + 1) * P]
    return t[:, rows, m * P:(m + 1) * P]


def at_k(w, k, cols=slice(None)):
    return (w[0][:, k, cols], w[1][:, k, cols]) if isinstance(w, tuple) else w[:, k, cols]


class Net:

    def __init__(self, nc, ctx, ins, out, known):
        self.nc, self.ins, self.out = nc, ins, out
        self.led = Ledger(nc, ctx, known)
        sb = lambda name, cols, dt=F32: ctx.enter_context(nc.sbuf_tensor(name, [P, cols], dt))
        self.ps = ctx.enter_context(nc.psum_tensor("psum", [P, 8, BANK], F32))
        with ExitStack() as names:
            self.ring_r = names.enter_context(nc.sbuf_tensor("weight_ring_low_halves", [P, SLOTS * SLOT], F32R))
            self.area_r = names.enter_context(nc.sbuf_tensor("stage_area_halves", [P, AREA_HALVES], F32R))
        self.ring = sb("weight_ring", SLOTS * SLOT)
        self.area = sb("stage_area", AREA)
        self.high_ring = sb("weight_high_halves", HIGH_SLOTS * SLOT, F32R)
        self.x_buf = sb("x", MT * D)
        self.ax_buf = sb("scaled_residual", MT * D)
        self.norm_buf = sb("norm_params", 2 * 2 * D)
        self.vfirst = sb("first_values", MT * 512)
        self.consts = sb("constants", CONST_COLS)
        self.small = sb("small", 1024)
        self.x = self.x_buf[:, :].rearrange("p (m n) -> p m n", m=MT)
        self.ax = self.ax_buf[:, :].rearrange("p (m n) -> p m n", m=MT)
        self.norms = self.norm_buf[:, :].rearrange("p (b g n) -> p b g n", b=2, g=2)
        self.stream, self.split_pieces = [], []
        self.groups = [0] * 8
        self.xT = self.part(0, KT, S)
        self.qT = self.part(2048, 8, S)
        self.kT = self.part(4096, 8, S)
        self.v_tok = self.part(6144, MT, D)
        self.probs = self.part(8192, 2, MT, S)
        self.pT = self.part(9216, 2, MT, S)
        self.oT = self.part(10240, KT, S)
        self.biased = self.part(12288, 2, MT, S)
        self.EXTRA = 13312
        self.ffn_sg = self.part(2048, MT, BANK)
        self.ffn_h = self.part(4096, 2, MT, BANK)
        self.xT_halves = (self.halves_part(0, KT, S), self.halves_part(7168, KT, S))
        self.ffn_hT = (self.halves_part(6144, 4, S), self.halves_part(9216, 4, S))
        self.small_at = 0
        self.ident = self.const("ident")

    def part(self, at, *dims):
        n = 1
        for d in dims:
            n *= d
        assert at + n <= AREA, (at, dims)
        ap = self.area[:, at:at + n]
        if len(dims) == 2:
            return ap.rearrange("p (a b) -> p a b", a=dims[0])
        if len(dims) == 3:
            return ap.rearrange("p (a b c) -> p a b c", a=dims[0], b=dims[1])
        if len(dims) == 4:
            return ap.rearrange("p (a b c d) -> p a b c d", a=dims[0], b=dims[1], c=dims[2])
        return ap

    def halves_part(self, at, a, b):
        return self.area_r[:, at:at + a * b].rearrange("p (a b) -> p a b", a=a)

    def tiny(self, *dims):
        n = int(np.prod(dims))
        at = self.small_at
        self.small_at += n
        assert self.small_at <= 1024
        ap = self.small[:, at:at + n]
        if len(dims) == 2:
            return ap.rearrange("p (a b) -> p a b", a=dims[0])
        return ap

    def const(self, name, *dims):
        at, n = CONST_AT[name]
        ap = self.consts[:, at:at + n]
        if len(dims) == 2:
            return ap.rearrange("p (a b) -> p a b", a=dims[0])
        return ap


    def piece(self, name, src, kts, n, split=False):
        assert kts * n <= SLOT
        index = sum(1 for e in self.stream if e[0] == "weights")
        self.stream.append(("weights", name, src, kts, n, index))
        if split:
            self.split_pieces.append(name)

    def load_param(self, name, dst, src, after=(), topic=None):
        self.stream.append(("param", name, dst, src, after, topic or "loaded_" + "_".join(map(str, name))))

    def stream_sync(self, sp):
        pieces = [e for e in self.stream if e[0] == "weights"]
        self.where = {e[1]: e for e in pieces}
        for e in self.stream:
            if e[0] == "param":
                _, name, dst, src, after, topic = e
                sp.wait_ge(*sp.at(*after))
                sp.raw.dma_start(dst, src).then_inc(*sp.mark(topic, ("loaded", name), *([("x", 0, m) for m in range(MT)] if name == ("x", 0) else []), by=16))
                continue
            _, name, src, kts, n, index = e
            slot = index % SLOTS
            if index >= SLOTS:
                sp.wait_ge(*sp.at(("used", pieces[index - SLOTS][1])))
            if isinstance(src, list):
                for j, (rows, at, cols, part) in enumerate(src):
                    dst = self.ring[rows, slot * SLOT + at:slot * SLOT + at + cols]
                    if len(part.shape) == 3:
                        dst = dst.rearrange("p (k n) -> p k n", k=part.shape[1])
                    names = [("loaded", name)] if j == len(src) - 1 else []
                    sp.raw.dma_start(dst, part).then_inc(*sp.mark(f"weights_in_slot{slot}", *names, by=16))
                continue
            dst = self.ring[:, slot * SLOT:slot * SLOT + kts * n].rearrange("p (k n) -> p k n", k=kts)
            sp.raw.dma_start(dst, src).then_inc(*sp.mark(f"weights_in_slot{slot}", ("loaded", name), by=16))

    def in_slot(self, name, ring=None, slot=None):
        _, _, _, kts, n, index = next(e for e in self.stream if e[1] == name)
        slot = index % SLOTS if slot is None else slot
        ring = self.ring if ring is None else ring
        return ring[:, slot * SLOT:slot * SLOT + kts * n].rearrange("p (k n) -> p k n", k=kts)

    def high_half(self, name):
        return self.in_slot(name, self.high_ring, self.split_pieces.index(name) % HIGH_SLOTS)

    def low_half(self, name):
        return self.in_slot(name, self.ring_r)

    def weights(self, pe, name):
        if name in self.split_pieces:
            pe.wait_ge(*pe.at(("halves", name)))
            return self.high_half(name), self.low_half(name)
        pe.wait_ge(*pe.at(("loaded", name)))
        return self.in_slot(name)

    def split_scalar(self, act, names):
        for name in names:
            i = self.split_pieces.index(name)
            act.wait_ge(*act.at(("loaded", name)))
            if i >= HIGH_SLOTS:
                act.wait_ge(*act.at(("used", self.split_pieces[i - HIGH_SLOTS])))
            act.raw.activation(self.high_half(name), self.in_slot(name), ACT.Copy).then_inc(*act.mark("high_halves", ("high", name)))

    def split_vector(self, v, names):
        for name in names:
            v.wait_ge(*v.at(("high", name)))
            v.raw.tensor_tensor(self.low_half(name), self.in_slot(name), self.high_half(name), ALU.subtract).then_inc(*v.mark("low_halves", ("halves", name)))

    def product(self, pe, out, a, w, start, stop):
        if isinstance(w, tuple):
            pe.raw.matmul(out, a[1], w[0], start=start, stop=False)
            pe.raw.matmul(out, a[0], w[1], start=False, stop=False)
            return pe.raw.matmul(out, a[0], w[0], start=False, stop=stop)
        return pe.raw.matmul(out, a, w, start=start, stop=stop)


    def free(self, bank):
        return [(f"psum{bank}_empty", self.groups[bank])] if self.groups[bank] else []

    def full(self, pe, bank, *events):
        self.groups[bank] += 1
        self.led.group_number[events[0]] = self.groups[bank]
        return pe.mark(f"psum{bank}_full", *events)

    def drained(self, eng, bank, group, *events):
        topic = f"psum{bank}_empty"
        self.led.drains.append((events, bank, group))
        if self.led.known is not None:
            eng.last = [self.led.known[("drained", group)]]
        return self.led.count(topic, (), 1)


    def plan_proj(self, tag, w, cols, kts):
        wv = w.rearrange("(k p) n -> p k n", p=P)
        for b, (c0, cn) in enumerate(cols):
            for h in range(kts // 4):
                self.piece((tag, b, h), wv[:, 4 * h:4 * h + 4, c0:c0 + cn], 4, cn)
        return dict(tag=tag, cols=cols, kts=kts)

    def proj_tensor(self, pe, pr, lhsT, bank, need=()):
        tag, kts = pr["tag"], pr["kts"]
        halves = kts // 4
        for b, (c0, cn) in enumerate(pr["cols"]):
            for m in range(MT):
                k_bank = bank(b, m)
                pe.wait_ge(*self.free(k_bank))
                if b == 0:
                    pe.wait_ge(*pe.at(*need[m] if need else ()))
                for k in range(kts):
                    w = self.weights(pe, (tag, b, k // 4))
                    mm = self.product(pe, self.ps[:, k_bank, 0:cn], lhsT(k, m), at_k(w, k % 4), k == 0, k == kts - 1)
                    if m == MT - 1 and k % 4 == 3 and k != kts - 1:
                        mm.then_inc(*pe.mark("weights_read", ("used", (tag, b, k // 4))))
                more = [("used", (tag, b, halves - 1))] if m == MT - 1 else []
                mm.then_inc(*self.full(pe, k_bank, (tag, "full", b, m), *more))

    def proj_copy(self, eng, pr, bank, take):
        tag = pr["tag"]
        for b, (c0, cn) in enumerate(pr["cols"]):
            for m in range(MT):
                who, copy = take(b, m)
                if who == eng.name:
                    eng.wait_ge(*eng.at((tag, "full", b, m)))
                    copy(eng, self.ps[:, bank(b, m), 0:cn]).then_inc(*self.drained(eng, bank(b, m), (tag, "full", b, m), (tag, "out", b, m)))

    def proj_names(self, pr):
        return [(pr["tag"], "out", b, m) for b in range(len(pr["cols"])) for m in range(MT)]

    def projT_tensor(self, pe, pr, rhs, banks, need=()):
        tag, kts = pr["tag"], pr["kts"]
        pe.wait_ge(*pe.at(*need))
        i = 0
        for b, (c0, cn) in enumerate(pr["cols"]):
            ws = [self.weights(pe, (tag, b, h)) for h in range(kts // 4)]
            for ct in range(cn // P):
                bank = banks[(i // 2) % len(banks)]
                if i % 2 == 0:
                    pe.wait_ge(*self.free(bank))
                for k in range(kts):
                    mm = pe.raw.matmul(self.ps[:, bank, (i % 2) * S:(i % 2) * S + S],
                                       ws[k // 4][:, k % 4, ct * P:(ct + 1) * P], rhs(k),
                                       start=(k == 0), stop=(k == kts - 1))
                last = ct == cn // P - 1
                more = [("used", (tag, b, h)) for h in range(kts // 4)] if last else []
                if i % 2 == 1:
                    mm.then_inc(*self.full(pe, bank, (tag, "full", i // 2), *more))
                i += 1

    def projT_copy(self, eng, pr, banks, dst, by, scale=1.0):
        tag = pr["tag"]
        n = sum(cn // P for _, cn in pr["cols"]) // 2
        for i in range(n):
            if by[i % len(by)] != eng.name:
                continue
            bank = banks[i % len(banks)]
            eng.wait_ge(*eng.at((tag, "full", i)))
            src = self.ps[:, bank, :].rearrange("p (a t) -> p a t", a=2)
            self.copy(eng, dst[:, 2 * i:2 * i + 2, :], src).then_inc(*self.drained(eng, bank, (tag, "full", i), (tag, "T", i)))

    def copy(self, eng, dst, src):
        if eng.name == "scalar":
            return eng.raw.activation(dst, src, ACT.Copy)
        return eng.raw.tensor_copy(dst, src)

    def halves_copy(self, eng, dst, src, bank, full, name):
        if eng.name == "scalar":
            eng.wait_ge(*eng.at(full))
            eng.raw.activation(dst[0], src, ACT.Copy).then_inc(*eng.mark("high_half_taken", (name, "high")))
        else:
            eng.wait_ge(*eng.at((name, "high")))
            eng.raw.tensor_tensor(dst[1], src, dst[0], ALU.subtract).then_inc(*self.drained(eng, bank, full, name))


    def turn_tensor(self, pe, groups):
        for g in groups:
            pe.wait_ge(*pe.at(*g["need"]))
            pe.wait_ge(*self.free(g["bank"]))
            for i, block in enumerate(g["blocks"]):
                mm = pe.raw.transpose(self.ps[:, g["bank"], i * P:(i + 1) * P], block, self.ident)
            mm.then_inc(*self.full(pe, g["bank"], (g["name"], "full")))

    def turn_copy(self, eng, groups):
        for g in groups:
            src = self.ps[:, g["bank"], 0:P * len(g["blocks"])].rearrange("p (i t) -> p i t", t=P)
            if isinstance(g["dst"], tuple):
                self.halves_copy(eng, g["dst"], src, g["bank"], (g["name"], "full"), g["name"])
                continue
            if g["by"] != eng.name:
                continue
            eng.wait_ge(*eng.at((g["name"], "full")))
            self.copy(eng, g["dst"], src).then_inc(*self.drained(eng, g["bank"], (g["name"], "full"), g["name"]))

    def turn_rows(self, tag, src, kts, dst, need, banks=(0, 1, 2, 3), by=("scalar", "vector")):
        groups = []
        i = 0
        for m in range(MT):
            for kg in range(0, kts, 4):
                groups.append(dict(name=(tag, m, kg), need=need(m), bank=banks[i % len(banks)],
                                   blocks=[src(m)[:, k * P:(k + 1) * P] for k in range(kg, kg + 4)],
                                   dst=pick(dst, slice(kg, kg + 4), m), by=by[i % len(by)]))
                i += 1
        return groups


    def rstd_gpsimd(self, pool, tag, src, dst):
        n = src.free_size()
        pool.wait_ge(*pool.at(("var", tag)))
        pool.raw.tensor_tensor(dst, src, self.const("minus_half")[:, 0:n], ALU.pow).then_inc(*pool.mark("rstd_ready", ("rstd", tag)))



def plan_ffn(net, tag, weights, chunks):
    gate_up, down = [], []
    order = []
    for c, cn in enumerate(chunks):
        wg, wu, wd = weights(c)
        for name, w in (("gate", wg), ("up", wu)):
            wv = w.rearrange("(k p) n -> p k n", p=P)
            for h in range(2):
                order.append((c, name, ((tag, name, c, h), wv[:, 4 * h:4 * h + 4, :], 4, cn)))
        dv = wd.rearrange("(k p) n -> p k n", p=P)
        for h, k0 in enumerate(range(0, cn // P, 2)):
            kn = min(2, cn // P - k0)
            order.append((c, "down", ((tag, "down", c, h), dv[:, k0:k0 + kn, :], kn, D)))
    for c in range(len(chunks) + 1):
        now = [p for cc, name, p in order if name != "down" and cc == c]
        for p in now + [p for cc, name, p in order if name == "down" and cc == c - 1]:
            net.piece(*p, split=True)
    names = lambda c, which: [p[0] for cc, name, p in order if cc == c and (name == "down") == (which == "down")]
    return dict(tag=tag, chunks=chunks, gate_up=[names(c, "gate_up") for c in range(len(chunks))],
                down=[names(c, "down") for c in range(len(chunks))])


def ffn_tensor(net, pe, f, need):
    tag, chunks = f["tag"], f["chunks"]

    def hidden(c, name, m):
        cn = chunks[c]
        bank = (0 if name == "gate" else 2) + m
        pe.wait_ge(*net.free(bank))
        if c == 0 and name == "gate":
            pe.wait_ge(*pe.at(*need[m]))
        for k in range(KT):
            w = net.weights(pe, (tag, name, c, k // 4))
            mm = net.product(pe, net.ps[:, bank, 0:cn], pick(net.xT_halves, k, m), at_k(w, k % 4), k == 0, k == KT - 1)
            if m == MT - 1 and k == 3:
                mm.then_inc(*pe.mark("weights_read", ("used", (tag, name, c, 0))))
        more = [("used", (tag, name, c, 1))] if m == MT - 1 else []
        mm.then_inc(*net.full(pe, bank, (tag, name, c, m), *more))

    def turn(c):
        for m in range(MT):
            pe.wait_ge(*pe.at((tag, "h", c, m)))
            pe.wait_ge(*net.free(m))
            for i in range(chunks[c] // P):
                mm = pe.raw.transpose(net.ps[:, m, i * P:(i + 1) * P],
                                      net.ffn_h[:, c % 2, m, i * P:(i + 1) * P], net.ident)
            mm.then_inc(*net.full(pe, m, (tag, "turned", c, m)))

    def down(c):
        if c == 0:
            for b in range(4, 8):
                pe.wait_ge(*net.free(b))
        kn = chunks[c] // P
        for i in range(kn):
            w = net.weights(pe, (tag, "down", c, i // 2))
            for m in range(MT):
                pe.wait_ge(*pe.at((tag, "hT", c, m)))
                for nb in range(2):
                    bank = 4 + 2 * m + nb
                    stop = c == len(chunks) - 1 and i == kn - 1
                    mm = net.product(pe, net.ps[:, bank, :], pick(net.ffn_hT, i, m),
                                     at_k(w, i % 2, slice(nb * BANK, (nb + 1) * BANK)), c == 0 and i == 0, stop)
                    last = m == MT - 1 and nb == 1 and (i % 2 == 1 or i == kn - 1)
                    more = [("used", (tag, "down", c, i // 2))] if last else []
                    if stop:
                        mm.then_inc(*net.full(pe, bank, (tag, "y", m, nb), *more))
                    elif last:
                        mm.then_inc(*pe.mark("weights_read", *more))

    for c in range(len(chunks) + 1):
        if c < len(chunks):
            hidden(c, "gate", 0)
            hidden(c, "gate", 1)
            hidden(c, "up", 0)
        if c >= 1:
            turn(c - 1)
        if c < len(chunks):
            hidden(c, "up", 1)
        if c >= 1:
            down(c - 1)


def ffn_scalar(net, act, f):
    tag, chunks = f["tag"], f["chunks"]

    def silu(c, m):
        cn = chunks[c]
        act.wait_ge(*act.at((tag, "gate", c, m)))
        if c >= 1:
            act.wait_ge(*act.at((tag, "h", c - 1, m)))
        act.raw.activation(net.ffn_sg[:, m, 0:cn], net.ps[:, m, 0:cn], ACT.Silu).then_inc(*net.drained(act, m, (tag, "gate", c, m), (tag, "silu", c, m)))

    for c in range(len(chunks) + 1):
        if c < len(chunks):
            silu(c, 0)
        if c >= 1:
            net.split_scalar(act, f["down"][c - 1])
        if c < len(chunks):
            silu(c, 1)
        if c >= 1:
            ffn_turned(net, act, f, c - 1)
        if c + 1 < len(chunks):
            net.split_scalar(act, f["gate_up"][c + 1])


def ffn_turned(net, eng, f, c):
    tag, n = f["tag"], f["chunks"][c] // P
    for m in range(MT):
        src = net.ps[:, m, 0:n * P].rearrange("p (i t) -> p i t", t=P)
        net.halves_copy(eng, pick(net.ffn_hT, slice(0, n), m), src, m, (tag, "turned", c, m), (tag, "hT", c, m))


def ffn_vector(net, v, f, scale=None):
    tag, chunks = f["tag"], f["chunks"]

    def mul(c, m):
        cn = chunks[c]
        v.wait_ge(*v.at((tag, "up", c, m), (tag, "silu", c, m)))
        if c >= 2:
            v.wait_ge(*v.at((tag, "turned", c - 2, m)))
        out, up, sg = net.ffn_h[:, c % 2, m, 0:cn], net.ps[:, 2 + m, 0:cn], net.ffn_sg[:, m, 0:cn]
        if scale:
            inst = v.raw.scalar_tensor_tensor(out=out, in0=up, scalar=scale(c, m), in1=sg, op0=ALU.mult, op1=ALU.mult)
        else:
            inst = v.raw.tensor_tensor(out, up, sg, ALU.mult)
        inst.then_inc(*net.drained(v, 2 + m, (tag, "up", c, m), (tag, "h", c, m)))

    for c in range(len(chunks) + 1):
        if c >= 1:
            net.split_vector(v, f["down"][c - 1])
        if c < len(chunks):
            mul(c, 0)
        if c >= 1:
            ffn_turned(net, v, f, c - 1)
        following = f["gate_up"][c + 1] if c + 1 < len(chunks) else []
        net.split_vector(v, following[:1])
        if c < len(chunks):
            mul(c, 1)
        net.split_vector(v, following[1:])



def attn_tensor(net, pe, tag, heads, per_group, need_q=(), need_v=()):
    n = len(heads)

    def scores(i):
        h = heads[i]
        bank = i % 2
        pe.wait_ge(*net.free(bank))
        if i == 0:
            pe.wait_ge(*pe.at(*need_q))
        for m in range(MT):
            for j in range(h["nk"]):
                mm = pe.raw.matmul(net.ps[:, bank, m * S:(m + 1) * S], h["q"](j, m), h["k"](j),
                                   start=(j == 0), stop=(j == h["nk"] - 1))
        mm.then_inc(*net.full(pe, bank, (tag, "scores", i)))

    def turn(i):
        bank = 2 + i % 2
        pe.wait_ge(*pe.at((tag, "probs", i)))
        pe.wait_ge(*net.free(bank))
        for kt in range(MT):
            for m in range(MT):
                mm = pe.raw.transpose(net.ps[:, bank, kt * S + m * P:kt * S + (m + 1) * P],
                                      net.probs[:, i % 2, m, kt * P:(kt + 1) * P], net.ident)
        mm.then_inc(*net.full(pe, bank, (tag, "turned", i)))

    def values(i):
        h = heads[i]
        g = i // per_group
        bank = 4 + g % 2
        pe.wait_ge(*pe.at((tag, "pT", i)))
        if i == 0:
            pe.wait_ge(*pe.at(*need_v))
        if i % per_group == 0:
            pe.wait_ge(*net.free(bank))
        for part, (p0, rows, ct) in enumerate(h["out"]):
            for kt in range(MT):
                mm = pe.raw.matmul(net.ps[p0:p0 + rows, bank, ct * S:(ct + 1) * S], h["v"](part, kt),
                                   net.pT[:, i % 2, kt, :], start=(kt == 0), stop=(kt == MT - 1))
        if i % per_group == per_group - 1:
            mm.then_inc(*net.full(pe, bank, (tag, "values", g)))

    for i in range(n + 2):
        if i < n:
            scores(i)
        if 1 <= i <= n:
            turn(i - 1)
        if i >= 2:
            values(i - 2)


def attn_vector(net, v, tag, heads, per_group, need_bias=()):
    n = len(heads)
    nmax, total, extra = net.nmax, net.total, net.extra

    def top(i):
        h = heads[i]
        b = i % 2
        v.wait_ge(*v.at((tag, "scores", i)))
        if i >= 2:
            v.wait_ge(*v.at((tag, "exp", i - 2)))
        src = net.ps[:, b, :].rearrange("p (m k) -> p m k", m=MT)
        scale = h["scale"]
        if h["bias"] is not None:
            v.wait_ge(*v.at(*h.get("need", ())))
            inst = v.raw.scalar_tensor_tensor(out=net.biased[:, b], in0=src, scalar=scale, in1=h["bias"],
                                              op0=ALU.mult, op1=ALU.add)
            inst.then_inc(*net.drained(v, b, (tag, "scores", i), (tag, "biased", i)))
            v.wait_ge(*v.at((tag, "biased", i)))
            src, scale = net.biased[:, b], 1.0
        v.raw.tensor_reduce(net.mx[:, b, :], src, AX, ALU.max).then_inc(*v.step())
        v.wait_ge(*v.last)
        if h["sink"] is not None:
            v.raw.tensor_scalar(net.mx[:, b, :], net.mx[:, b, :], scale, h["sink"], ALU.mult, ALU.max).then_inc(*v.step())
            v.wait_ge(*v.last)
            scale = 1.0
            v.raw.tensor_scalar(nmax[:, b, :], net.mx[:, b, :], -1.0, None, ALU.mult).then_inc(*v.step())
            v.wait_ge(*v.last)
            v.raw.tensor_scalar(extra[:, b, :], nmax[:, b, :], h["sink"], None, ALU.add).then_inc(*v.mark("row_max_ready", (tag, "max", i)))
        else:
            v.raw.tensor_scalar(nmax[:, b, :], net.mx[:, b, :], -scale, None, ALU.mult).then_inc(*v.mark("row_max_ready", (tag, "max", i)))

    def normalise(i):
        b = i % 2
        v.wait_ge(*v.at((tag, "exp", i)))
        if heads[i]["sink"] is not None:
            v.raw.tensor_tensor(total[:, b, :], total[:, b, :], extra[:, b, :], ALU.add).then_inc(*v.step())
            v.wait_ge(*v.last)
        v.raw.reciprocal(net.inv[:, b, :], total[:, b, :]).then_inc(*v.step())
        v.wait_ge(*v.last)
        v.raw.tensor_scalar(net.probs[:, b, 0, :], net.probs[:, b, 0, :], net.inv[:, b, 0:1], None, ALU.mult)
        v.raw.tensor_scalar(net.probs[:, b, 1, :], net.probs[:, b, 1, :], net.inv[:, b, 1:2], None, ALU.mult).then_inc(*v.mark("probs_ready", (tag, "probs", i)))

    def out(g):
        v.wait_ge(*v.at((tag, "values", g)))
        src = net.ps[:, 4 + g % 2, :].rearrange("p (a t) -> p a t", a=2)
        v.raw.tensor_copy(net.oT[:, 2 * g:2 * g + 2, :], src).then_inc(*net.drained(v, 4 + g % 2, (tag, "values", g), (tag, "oT", g)))

    for i in range(n + 4):
        if i < n:
            top(i)
        if 1 <= i <= n:
            normalise(i - 1)
        if i >= 3 and (i - 3) % per_group == per_group - 1 and i - 3 < n:
            out((i - 3) // per_group)


def attn_scalar(net, act, tag, heads):
    n = len(heads)

    def exps(i):
        b = i % 2
        h = heads[i]
        act.wait_ge(*act.at((tag, "max", i)))
        if h["bias"] is None:
            act.wait_ge(*act.at((tag, "scores", i)))
        if i >= 2:
            act.wait_ge(*act.at((tag, "turned", i - 2)))
        for m in range(MT):
            if h["bias"] is not None:
                src, scale = net.biased[:, b, m, :], 1.0
            else:
                src, scale = net.ps[:, b, m * S:(m + 1) * S], h["scale"]
            inst = act.raw.activation(net.probs[:, b, m, :], src, ACT.Exp, bias=net.nmax[:, b, m:m + 1],
                                      scale=scale, accum_out=net.total[:, b, m:m + 1])
        if h["sink"] is not None:
            if h["bias"] is None:
                inst.then_inc(*net.drained(act, b, (tag, "scores", i)))
            inst = act.raw.activation(net.extra[:, b, :], net.extra[:, b, :], ACT.Exp)
            inst.then_inc(*act.mark("exp_done", (tag, "exp", i)))
        elif h["bias"] is None:
            inst.then_inc(*net.drained(act, b, (tag, "scores", i), (tag, "exp", i)))
        else:
            inst.then_inc(*act.mark("exp_done", (tag, "exp", i)))

    def turned(i):
        act.wait_ge(*act.at((tag, "turned", i)))
        src = net.ps[:, 2 + i % 2, :].rearrange("p (k t) -> p k t", k=MT)
        act.raw.activation(net.pT[:, i % 2], src, ACT.Copy).then_inc(*net.drained(act, 2 + i % 2, (tag, "turned", i), (tag, "pT", i)))

    for i in range(n + 1):
        if i < n:
            exps(i)
        if i >= 1:
            turned(i - 1)


def head(q, k, v, out, scale, nk=1, bias=None, sink=None, need=()):
    return dict(q=q, k=k, v=v, out=out, scale=scale, nk=nk, bias=bias, sink=sink, need=need)



def residual_scalar(net, act, n):
    for m in range(MT):
        act.wait_ge(*act.at(("x", n, m)))
        act.raw.activation(net.ax[:, m, :], net.x[:, m, :], ACT.Copy, scale=ALPHA).then_inc(*act.mark("residual_scaled", ("ax", n, m)))


def ln_vector(net, v, n, coef, y_names):
    for m in range(MT):
        x = net.x[:, m, :]
        g, b = net.norms[:, n % 2, 0, :], net.norms[:, n % 2, 1, :]
        v.wait_ge(*v.at(("ax", n, m), *y_names(m)))
        for nb in range(2):
            cols = slice(nb * BANK, (nb + 1) * BANK)
            inst = v.raw.scalar_tensor_tensor(out=x[:, cols], in0=net.ps[:, 4 + 2 * m + nb, :], scalar=coef,
                                              in1=net.ax[:, m, cols], op0=ALU.mult, op1=ALU.add)
            inst.then_inc(*net.drained(v, 4 + 2 * m + nb, y_names(m)[nb]))
        v.wait_ge(*v.last)
        for nb in range(2):
            v.raw.bn_stats(net.bn[:, m, 6 * nb:6 * nb + 6], x[:, nb * BANK:(nb + 1) * BANK]).then_inc(*v.step())
            v.wait_ge(*v.last)
        v.raw.bn_aggr(net.mv[:, m, :], net.bn[:, m, :]).then_inc(*v.step())
        v.wait_ge(*v.last)
        v.raw.tensor_scalar(net.var[:, m:m + 1], net.mv[:, m, 1:2], LN_EPS, None, ALU.add).then_inc(*v.mark("variance_ready", ("var", ("ln", n, m))))
        v.wait_ge(*v.at(("loaded", ("norm", n))))
        v.raw.scalar_tensor_tensor(out=x, in0=x, scalar=net.mv[:, m, 0:1], in1=g, op0=ALU.subtract, op1=ALU.mult).then_inc(*v.step())
        v.wait_ge(*v.last)
        v.wait_ge(*v.at(("rstd", ("ln", n, m))))
        v.raw.scalar_tensor_tensor(out=x, in0=x, scalar=net.rstd[:, m:m + 1], in1=b, op0=ALU.mult, op1=ALU.add).then_inc(*v.mark("x_ready", ("x", n + 1, m)))


def ln_gpsimd(net, pool, n):
    for m in range(MT):
        net.rstd_gpsimd(pool, ("ln", n, m), net.var[:, m:m + 1], net.rstd[:, m:m + 1])


def row_broadcast(ap, n):
    return bass.AP(ap.tensor, ap.offset, [[0, P], [1, n]])


def widen(ap, at, n):
    dims = [list(d) for d in ap.ap]
    dims.insert(at, [0, n])
    return bass.AP(ap.tensor, ap.offset, dims)



def rope(eng, raw, x, cos, sin, temps, done):
    heads = x.shape[2]
    x1, x2 = x[:, :, :, 0:32], x[:, :, :, 32:64]
    c, s = widen(cos, 2, heads), widen(sin, 2, heads)
    t1, t2 = temps
    raw.tensor_tensor(t1, x1, s, ALU.mult)
    raw.tensor_tensor(t2, x2, s, ALU.mult).then_inc(*eng.step())
    eng.wait_ge(*eng.last)
    raw.tensor_tensor(x1, x1, c, ALU.mult)
    raw.tensor_tensor(x2, x2, c, ALU.mult).then_inc(*eng.step())
    eng.wait_ge(*eng.last)
    raw.tensor_tensor(x1, x1, t2, ALU.subtract)
    raw.tensor_tensor(x2, x2, t1, ALU.add).then_inc(*eng.mark(*done))


def blocks(n, width=BANK):
    return [(c, min(width, n - c)) for c in range(0, n, width)]


class First:

    def __init__(self, net):
        self.net = net
        ins = net.ins
        net.mx, net.nmax = net.tiny(2, MT), net.tiny(2, MT)
        net.total, net.extra, net.inv = net.tiny(2, MT), net.tiny(2, MT), net.tiny(2, MT)
        net.bn, net.mv = net.tiny(MT, 12), net.tiny(MT, 2)
        net.var, net.rstd = net.tiny(MT), net.tiny(MT)
        self.sink = net.tiny(8)
        self.gains = net.tiny(2, HD)
        self.ssum, self.srstd = net.tiny(20), net.tiny(20)
        E = net.EXTRA
        self.memT = net.part(18944, KT, S)
        self.mem_tok = net.part(E, MT, D)
        self.qkv = net.part(E, MT, 1536)
        self.tA = net.part(E + 3072, MT, 640)
        self.tB = net.part(E + 3072 + 1280, MT, 640)
        self.kdup = net.part(6144, MT, 4, P)
        self.bias = net.part(E, 2, MT, 4 * S)
        tok = lambda a: a.rearrange("b (m p) n -> p (b m) n", p=P)
        net.load_param(("x", 0), net.x, tok(ins["x"]))
        net.load_param(("const", 0), net.consts[:, :], ins["constants"])
        net.load_param(("mem", 0), self.mem_tok, tok(ins["mem"]))
        self.load_norm(0)
        self.load_norm(1)
        net.load_param(("ab", "sink"), self.sink, row_broadcast(ins["ab_sink"], 8))
        net.load_param(("ab", "q"), self.gains[:, 0, :], row_broadcast(ins["ab_q_gain"], HD))
        net.load_param(("ab", "k"), self.gains[:, 1, :], row_broadcast(ins["ab_k_gain"], HD))
        self.stages = []
        net.skew = net.nc.dram_tensor("bias_rows", (16, 7, GRID_W, self.LINE), F32, kind="Internal").ap()
        for i in range(2):
            st = {}
            st["ffn0"] = self.plan_ffn(i, 0)
            if i == 1:
                self.load_norm(5)
            if i == 0:
                st["ab_in"] = net.plan_proj("ab_in", ins["ab_w_in"][0], blocks(1536), KT)
                st["mix_out"] = net.plan_proj("ab_out", ins["ab_w_out"][0], blocks(D), KT)
            else:
                w = ins["c_w_in"][0]
                for h in range(16):
                    self.store_skew(h)
                st["c_q"] = net.plan_proj("c_q", w[:, 0:D], blocks(D), KT)
                st["c_k"] = net.plan_proj("c_k", w[:, D:2 * D], blocks(D), KT)
                self.load_bias(0)
                self.load_bias(1)
                st["c_v"] = net.plan_proj("c_v", w[:, 2 * D:3 * D], blocks(D), KT)
                self.load_bias(2)
                self.load_bias(3)
                st["mix_out"] = net.plan_proj("c_out", ins["c_w_out"][0], blocks(D), KT)
            wkv = ins["mem_w_kv"][i]
            st["mk"] = net.plan_proj(f"mem{i}_k", wkv[:, 0:D], blocks(D), KT)
            st["mv"] = net.plan_proj(f"mem{i}_v", wkv[:, D:2 * D], blocks(D), KT)
            self.load_norm(4 * i + 2)
            st["mq"] = net.plan_proj(f"mem{i}_q", ins["mem_w_q"][i], blocks(D), KT)
            st["mo"] = net.plan_proj(f"mem{i}_o", ins["mem_w_o"][i], blocks(D), KT)
            self.load_norm(4 * i + 3)
            st["ffn1"] = self.plan_ffn(i, 1)
            if i == 0:
                self.load_norm(4)
            self.stages.append(st)

    def load_norm(self, n):
        net = self.net
        i, j = n // 4, n % 4
        after = [("x", n - 1, 1)] if n >= 2 else []
        net.load_param(("norm_g", n), net.norms[:, n % 2, 0, :], row_broadcast(net.ins["ln_g"][i, j], D), after,
                       topic=f"loaded_norm{n % 2}")
        net.load_param(("norm", n), net.norms[:, n % 2, 1, :], row_broadcast(net.ins["ln_b"][i, j], D), after,
                       topic=f"loaded_norm{n % 2}")

    def load_bias(self, g):
        net = self.net
        after = [("c", "biased", 4 * (g - 1) - 1)] if g >= 2 else []
        after = after + [("loaded", ("skew", 15))]
        skew = net.skew
        for m in range(MT):
            for r2 in range(2):
                r = 2 * m + r2
                for h in range(4):
                    at = ((4 * g + h) * 7 + 3 - r) * GRID_W * self.LINE + GRID_W - 1
                    src = bass.AP(skew.tensor, at, [[self.LINE - 1, GRID_W], [GRID_W * self.LINE, 4], [1, GRID_W]])
                    dst = self.bias[64 * r2:64 * r2 + 64, g % 2, m, h * S:(h + 1) * S]
                    net.load_param(("bias", g, m, r2, h), dst.rearrange("p (r w) -> p r w", r=4), src, after,
                                   topic=f"loaded_bias{g % 2}")

    LINE = 2 * GRID_W - 1

    def store_skew(self, h):
        net = self.net
        rpb = net.ins["c_rpb"]
        src = bass.AP(rpb.tensor, h * 465 + 4 * 31 + 15 - (GRID_W - 1), [[31, 7], [0, GRID_W], [1, self.LINE]])
        net.load_param(("skew", h), net.skew[h], src, topic="bias_rows_stored")

    def plan_ffn(self, i, j):
        ins = self.net.ins
        wg, wu, wd = ins["ffn_w_gate"][i, j], ins["ffn_w_up"][i, j], ins["ffn_w_down"][i, j]
        cols = blocks(D_FF)

        def weights(c):
            c0, cn = cols[c]
            return wg[:, c0:c0 + cn], wu[:, c0:c0 + cn], wd[c0:c0 + cn, :]

        return plan_ffn(self.net, f"ffn{i}{j}", weights, [cn for _, cn in cols])


    def ab_heads(self):
        net, out = self.net, []
        for which in range(2):
            for h in range(8):
                kv = h // 4
                rows = slice(64 * (h % 2), 64 * (h % 2) + 64)
                tile = 4 * which + h // 2
                v0 = (640 if which == 0 else 1408) + 64 * kv
                out.append(head(
                    q=lambda j, m, rows=rows, tile=tile: net.qT[rows, tile, m * P:(m + 1) * P],
                    k=lambda j, rows=rows, t=2 * which + kv: net.kT[rows, t, :],
                    v=lambda part, kt, v0=v0: self.qkv[:, kt, v0:v0 + 64],
                    out=[(64 * (h % 2), 64, h // 2 % 2)], scale=HD ** -0.5,
                    bias=net.const("window", MT, S) if which else None,
                    sink=self.sink[:, h:h + 1] if which else None,
                    need=[("loaded", ("ab", "sink"))] if which else []))
        return out

    def c_heads(self):
        net, out = self.net, []
        for h in range(16):
            rows = slice(64 * (h % 2), 64 * (h % 2) + 64)
            out.append(head(
                q=lambda j, m, rows=rows, h=h: net.qT[rows, h // 2, m * P:(m + 1) * P],
                k=lambda j, rows=rows, h=h: net.kT[rows, h // 2, :],
                v=lambda part, kt, h=h: net.v_tok[:, kt, 64 * h:64 * h + 64],
                out=[(64 * (h % 2), 64, h // 2 % 2)], scale=HD ** -0.5,
                bias=self.bias[:, h // 4 % 2, :, :].rearrange("p m (h k) -> p m h k", h=4)[:, :, h % 4, :],
                need=[("masked", h // 4)]))
        return out

    def mem_heads(self):
        net, out = self.net, []
        for h in range(4):
            out.append(head(
                q=lambda j, m, h=h: net.qT[:, 2 * h + j, m * P:(m + 1) * P],
                k=lambda j, h=h: net.kT[:, 2 * h + j, :],
                v=lambda part, kt, h=h: net.v_tok[:, kt, 256 * h + P * part:256 * h + P * (part + 1)],
                out=[(0, P, 0), (0, P, 1)], scale=256 ** -0.5, nk=2))
        return out


    def x_turn(self, n):
        return self.net.turn_rows(("xT", n), lambda m: self.net.x[:, m, :], KT,
                                  self.net.xT_halves if n % 4 in (0, 3) else self.net.xT,
                                  lambda m: [("x", n, m), ("loaded", ("const", 0))])

    def xT_need(self, n):
        return [[(("xT", n), m, kg) for kg in (0, 4)] for m in range(MT)]

    def mem_turn(self):
        return self.net.turn_rows("memT", lambda m: self.mem_tok[:, m, :], KT, self.memT,
                                  lambda m: [("loaded", ("mem", 0)), ("loaded", ("const", 0))])

    def ab_turn(self):
        net, groups = self.net, []
        for which in range(2):
            base = 768 * which
            ready = [("ab", "ready", which)]
            for m in range(MT):
                groups.append(dict(name=("ab", "qT", which, m), need=ready, bank=2 * which + m,
                                   blocks=[self.qkv[:, m, base + t * P:base + (t + 1) * P] for t in range(4)],
                                   dst=net.qT[:, 4 * which:4 * which + 4, m * P:(m + 1) * P],
                                   by="scalar" if m else "vector"))
            groups.append(dict(name=("ab", "kT", which), need=ready, bank=2 * which,
                               blocks=[self.kdup[:, m, 2 * which + kv, :] for kv in range(2) for m in range(MT)],
                               dst=net.kT[:, 2 * which:2 * which + 2, :].rearrange("p w (m t) -> p (w m) t", m=MT),
                               by="scalar"))
        return groups


    def out_bank(self, b, m):
        return 4 + 2 * m + b

    def tensor(self, pe):
        net = self.net
        oT = lambda k, m: net.oT[:, k, m * P:(m + 1) * P]
        xT = lambda k, m: net.xT[:, k, m * P:(m + 1) * P]
        rot = lambda b, m: (2 * b + m) % 4
        net.turn_tensor(pe, self.mem_turn())
        for i, st in enumerate(self.stages):
            n = 4 * i
            net.turn_tensor(pe, self.x_turn(n))
            ffn_tensor(net, pe, st["ffn0"], self.xT_need(n))
            net.turn_tensor(pe, self.x_turn(n + 1))
            need = self.xT_need(n + 1)
            if i == 0:
                net.proj_tensor(pe, st["ab_in"], xT, rot, need)
                net.turn_tensor(pe, self.ab_turn())
                turned = [g["name"] for g in self.ab_turn()]
                attn_tensor(net, pe, "ab", self.ab_heads(), 4, need_q=turned)
                groups, tag = 4, "ab"
            else:
                net.projT_tensor(pe, st["c_q"], lambda k: net.xT[:, k, :], range(4), need[0] + need[1])
                net.projT_tensor(pe, st["c_k"], lambda k: net.xT[:, k, :], range(4))
                net.proj_tensor(pe, st["c_v"], xT, rot)
                attn_tensor(net, pe, "c", self.c_heads(), 4,
                            need_q=[(t, "T", g) for t in ("c_q", "c_k") for g in range(4)],
                            need_v=net.proj_names(st["c_v"]))
                groups, tag = 4, "c"
            done = [(tag, "oT", g) for g in range(groups)]
            net.proj_tensor(pe, st["mix_out"], oT, self.out_bank, [done, done])
            net.projT_tensor(pe, st["mk"], lambda k: self.memT[:, k, :], range(4),
                             [("memT", m, kg) for m in range(MT) for kg in (0, 4)])
            net.proj_tensor(pe, st["mv"], lambda k, m: self.memT[:, k, m * P:(m + 1) * P], rot)
            net.turn_tensor(pe, self.x_turn(n + 2))
            need = self.xT_need(n + 2)
            net.projT_tensor(pe, st["mq"], lambda k: net.xT[:, k, :], range(4), need[0] + need[1])
            tag = f"mem{i}"
            attn_tensor(net, pe, tag, self.mem_heads(), 1,
                        need_q=[(f"mem{i}_{t}", "T", g) for t in "qk" for g in range(4)],
                        need_v=net.proj_names(st["mv"]))
            done = [(tag, "oT", g) for g in range(4)]
            net.proj_tensor(pe, st["mo"], oT, self.out_bank, [done, done])
            net.turn_tensor(pe, self.x_turn(n + 3))
            ffn_tensor(net, pe, st["ffn1"], self.xT_need(n + 3))


    def v_take(self, b, m):
        net = self.net
        return "scalar", lambda e, ps: net.copy(e, net.v_tok[:, m, b * BANK:(b + 1) * BANK], ps)

    def ab_take(self, b, m):
        net = self.net
        return ("scalar" if m else "vector",
                lambda e, ps: net.copy(e, self.qkv[:, m, b * BANK:(b + 1) * BANK], ps))

    def y_names(self, tag):
        return lambda m: [(tag, "full", b, m) for b in range(2)]

    def scalar(self, act):
        net = self.net
        rot = lambda b, m: (2 * b + m) % 4
        act.wait_ge(*act.at(("loaded", ("x", 0))))
        net.turn_copy(act, self.mem_turn())
        for i, st in enumerate(self.stages):
            n = 4 * i
            first = st["ffn0"]["gate_up"][0]
            net.split_scalar(act, first[:2] if i else [])
            net.turn_copy(act, self.x_turn(n))
            net.split_scalar(act, first[2:] if i else first)
            residual_scalar(net, act, n)
            ffn_scalar(net, act, st["ffn0"])
            net.turn_copy(act, self.x_turn(n + 1))
            residual_scalar(net, act, n + 1)
            if i == 0:
                net.proj_copy(act, st["ab_in"], rot, self.ab_take)
                net.turn_copy(act, self.ab_turn())
                attn_scalar(net, act, "ab", self.ab_heads())
            else:
                net.projT_copy(act, st["c_q"], range(4), net.qT, ["scalar"])
                net.projT_copy(act, st["c_k"], range(4), net.kT, ["scalar"])
                net.proj_copy(act, st["c_v"], rot, self.v_take)
                attn_scalar(net, act, "c", self.c_heads())
            net.projT_copy(act, st["mk"], range(4), net.kT, ["scalar"])
            net.proj_copy(act, st["mv"], rot, self.v_take)
            net.turn_copy(act, self.x_turn(n + 2))
            residual_scalar(net, act, n + 2)
            net.projT_copy(act, st["mq"], range(4), net.qT, ["scalar"])
            attn_scalar(net, act, f"mem{i}", self.mem_heads())
            net.split_scalar(act, st["ffn1"]["gate_up"][0][:2])
            net.turn_copy(act, self.x_turn(n + 3))
            net.split_scalar(act, st["ffn1"]["gate_up"][0][2:])
            residual_scalar(net, act, n + 3)
            ffn_scalar(net, act, st["ffn1"])

    def ab_vector(self, v):
        net = self.net
        v.wait_ge(*v.at(*net.proj_names(self.stages[0]["ab_in"])))
        for m in range(MT):
            x = self.qkv[:, m, 0:640]
            v.raw.tensor_tensor(self.tA[:, m, :], x, x, ALU.mult).then_inc(*v.step())
            v.wait_ge(*v.last)
        v.raw.tensor_reduce(self.ssum, self.tA.rearrange("p m (h d) -> p (m h) d", d=HD), AX, ALU.add).then_inc(*v.step())
        v.wait_ge(*v.last)
        v.raw.tensor_scalar(self.ssum, self.ssum, 1.0 / HD, RMS_EPS, ALU.mult, ALU.add).then_inc(*v.mark("variance_ready", ("var", "ab")))
        v.wait_ge(*v.at(("loaded", ("ab", "q")), ("loaded", ("ab", "k")), ("rstd", "ab")))
        for m in range(MT):
            x = self.qkv[:, m, 0:640].rearrange("p (h d) -> p h d", d=HD)
            v.raw.tensor_tensor(x, x, widen(self.srstd[:, 10 * m:10 * m + 10], 2, HD), ALU.mult).then_inc(*v.step())
            v.wait_ge(*v.last)
            v.raw.tensor_tensor(x[:, 0:8, :], x[:, 0:8, :], widen(self.gains[:, 0, :], 1, 8), ALU.mult)
            v.raw.tensor_tensor(x[:, 8:10, :], x[:, 8:10, :], widen(self.gains[:, 1, :], 1, 2), ALU.mult).then_inc(*v.step())
            v.wait_ge(*v.last)
        temps = [self.tA[:, :, h * 320:(h + 1) * 320].rearrange("p m (h d) -> p m h d", d=32) for h in range(2)]
        rope(v, v.raw, self.qkv[:, :, 0:640].rearrange("p m (h d) -> p m h d", d=HD),
             net.const("cos2", MT, 32), net.const("sin2", MT, 32), temps, ("heads_turned", ("ab", "rope", 0)))
        self.double_keys(v, 0, "heads_ready")

    def double_keys(self, eng, which, topic):
        eng.wait_ge(*eng.at(("ab", "rope", which)))
        for m in range(MT):
            k = self.qkv[:, m, 768 * which + 512:768 * which + 640].rearrange("p (k d) -> p k d", d=HD)
            dst = self.kdup[:, m, 2 * which:2 * which + 2, :].rearrange("p k (e d) -> p k e d", e=2)
            inst = eng.raw.tensor_copy(dst, widen(k, 2, 2))
        inst.then_inc(*eng.mark(topic, ("ab", "ready", which)))

    def vector(self, v):
        net = self.net
        net.turn_copy(v, self.mem_turn())
        for i, st in enumerate(self.stages):
            n = 4 * i
            net.turn_copy(v, self.x_turn(n))
            net.split_vector(v, st["ffn0"]["gate_up"][0][2 if i else 0:])
            f = st["ffn0"]
            ffn_vector(net, v, f)
            ln_vector(net, v, n, 0.5, lambda m, t=f["tag"]: [(t, "y", m, nb) for nb in range(2)])
            net.turn_copy(v, self.x_turn(n + 1))
            if i == 0:
                net.proj_copy(v, st["ab_in"], lambda b, m: (2 * b + m) % 4, self.ab_take)
                self.ab_vector(v)
                net.turn_copy(v, self.ab_turn())
                attn_vector(net, v, "ab", self.ab_heads(), 4)
            else:
                attn_vector(net, v, "c", self.c_heads(), 4)
            ln_vector(net, v, n + 1, 1.0, self.y_names(st["mix_out"]["tag"]))
            net.turn_copy(v, self.x_turn(n + 2))
            attn_vector(net, v, f"mem{i}", self.mem_heads(), 1)
            net.split_vector(v, st["ffn1"]["gate_up"][0][:2])
            ln_vector(net, v, n + 2, 1.0, self.y_names(st["mo"]["tag"]))
            net.turn_copy(v, self.x_turn(n + 3))
            net.split_vector(v, st["ffn1"]["gate_up"][0][2:])
            f = st["ffn1"]
            ffn_vector(net, v, f)
            if i == 0:
                net.split_vector(v, self.stages[1]["ffn0"]["gate_up"][0][:2])
            ln_vector(net, v, n + 3, 0.5, lambda m, t=f["tag"]: [(t, "y", m, nb) for nb in range(2)])

    def gpsimd(self, pool):
        net = self.net
        pool.wait_ge(*pool.at(("loaded", ("const", 0))))
        for i, st in enumerate(self.stages):
            n = 4 * i
            ln_gpsimd(net, pool, n)
            if i == 0:
                pool.wait_ge(*pool.at(*net.proj_names(st["ab_in"])))
                temps = [self.tB[:, :, h * 320:(h + 1) * 320].rearrange("p m (h d) -> p m h d", d=32) for h in range(2)]
                net.rstd_gpsimd(pool, "ab", self.ssum, self.srstd)
                rope(pool, pool.raw, self.qkv[:, :, 768:1408].rearrange("p m (h d) -> p m h d", d=HD),
                     net.const("cos1", MT, 32), net.const("sin1", MT, 32), temps,
                     ("window_heads_turned", ("ab", "rope", 1)))
                self.double_keys(pool, 1, "window_heads_ready")
            else:
                for g in range(4):
                    pool.wait_ge(*pool.at(("loaded", ("bias", g, MT - 1, 1, 3))))
                    for m in range(MT):
                        b = self.bias[:, g % 2, m, :].rearrange("p (h k) -> p h k", h=4)
                        inst = pool.raw.tensor_tensor(b, b, widen(net.const("columns", MT, S)[:, m, :], 1, 4), ALU.add)
                    inst.then_inc(*pool.mark("bias_masked", ("masked", g)))
            ln_gpsimd(net, pool, n + 1)
            ln_gpsimd(net, pool, n + 2)
            ln_gpsimd(net, pool, n + 3)


DECAY = float(np.exp(np.float32(-0.5)))
LNX_EPS = 1e-5 * HD
NORM_EPS = 1e-6
N_A, N_B = 1792, 1224
TAKEN = -3e38


class Second:

    def __init__(self, net, x0):
        self.net, self.x0 = net, x0
        ins = net.ins
        if not hasattr(net, "mx"):
            net.mx, net.nmax = net.tiny(2, MT), net.tiny(2, MT)
            net.total, net.extra, net.inv = net.tiny(2, MT), net.tiny(2, MT), net.tiny(2, MT)
        self.sq, self.row_rstd = net.tiny(MT), net.tiny(MT)
        self.pos_i, self.pos = net.tiny(MT), net.tiny(MT)
        self.angle, self.turns = net.tiny(MT, 32), net.tiny(MT, 32)
        self.cos, self.sin = net.tiny(MT, 32), net.tiny(MT, 32)
        self.hs, self.hr = net.tiny(32), net.tiny(32)
        self.w_idx = net.tiny(MT, 8)
        self.top8 = net.tiny(8)
        self.bonus = net.tiny(MT, 8)
        self.decay_end = net.tiny(4, 4)
        self.logits, self.gates = net.tiny(MT, 8), net.tiny(MT, 8)
        self.gate_sum = net.tiny(MT)
        self.router_bias = net.tiny(8)
        E = net.EXTRA
        self.colsB = net.part(E, MT, N_B)
        self.score = net.part(E + 2448, MT, S)
        self.work = net.part(E + 2960, MT, S)
        self.relu = net.part(E + 3472, 2, MT, S)
        self.chosen = net.part(E + 4496, MT, S)
        self.kdup = net.part(E + 5008, MT, 2, P)
        self.ropeA = net.part(E + 5520, MT, 288)
        self.ropeB = net.part(E + 6096, MT, 288)
        self.dsa_gain = net.part(20480, 3, HD)
        self.colsA = net.part(4608, MT, N_A)
        self.colsS = net.part(E, MT, N_A)
        self.mu = net.part(16896, N_A)
        rows = lambda at: net.part(at, MT, 512)
        self.sig, self.a, self.g, self.kk = rows(2048), rows(3072), rows(8192), rows(9216)
        self.wadT, self.gdT = net.part(4096, S), net.part(4352, S)
        self.decay, self.undecay = rows(11264), rows(12288)
        self.vec = net.part(E, 8, 512)
        self.at, self.bh, self.tmp = rows(17408), rows(18432), rows(19456)
        self.vT, self.vv = net.part(17408, 4, S), net.part(20480, S)
        self.r, self.k, self.v = (self.colsA[:, :, i * 512:(i + 1) * 512] for i in range(3))
        self.arT = net.part(2048, 4, MT, S)
        self.bT, self.khT = net.part(9216, 4, S), net.part(11264, 4, S)
        self.packed = net.part(E, 16, 3, CH)
        self.solve = net.part(12288, 16, CH)
        group = lambda ap, at: ap[:, at:at + BANK].rearrange("p (q t) -> p q t", q=4)
        self.LT = [group(net.area, 17408), group(net.ax_buf, 0)]
        self.X = [group(net.area, 17920), group(net.ax_buf, 512)]
        self.Y = [group(net.area, 19456), group(net.ax_buf, 1024)]
        self.W = [group(net.area, 19968), group(net.ax_buf, 1536)]
        self.rhs, self.sa = rows(17408), self.colsA[:, :, 0:512]
        self.state = [net.part(9216, 4, P), net.part(9728, 4, P)]
        self.v_half = net.ax_buf[:, :].rearrange("p (e m n) -> p e m n", e=2, m=MT)
        self.y = rows(19456)
        self.yaT, self.ybT = net.part(11264, 4, S), net.part(10240, 4, S)
        self.gate = [net.part(E, MT, D), net.part(E + 2048, MT, D)]
        self.merged = net.part(E + 4096, MT, D)
        self.mergedT = net.part(2048, KT, S)
        self.mem_tok = net.part(E, MT, D)
        self.memT = net.part(E + 2048, KT, S)
        self.q_tok = net.part(17408, MT, 512)
        self.sq_tok = net.part(18432, MT, 512)
        self.sk_tok = net.part(19456, MT, 512)
        self.mem_gain = net.part(20480, 2, P)

        for m in range(MT):
            net.load_param(("positions", m), self.pos_i[:, m:m + 1].bitcast(I32),
                           ins["positions_2"][:, m * P:(m + 1) * P].rearrange("b (p o) -> p (b o)", o=1), topic="loaded_positions")
        self.layers = []
        for l in range(2):
            st = {}
            self.load_rows(("mix", l), 0, ins["norm_mix_2"][l], [("hn", ("mix", l - 1), 1)] if l else [("x", x0, 1)])
            self.load_rows(("memx", l), 1, ins["norm_mem_2"][l], [("hn", ("memx", l - 1), 1)] if l else [("x", x0, 1)])
            self.load_rows(("memt", l), 2, ins["mem_tok_norm_2"][l], [("hn", ("memt", l - 1), 1)] if l else [("x", x0, 1)])
            self.load_rows(("ffn", l), 3, ins["norm_ffn_2"][l], [("hn", ("ffn", l - 1), 1)] if l else [("x", x0, 1)])
            for j, name in enumerate(("dsa_q_norm_2", "dsa_k_norm_2", "idx_k_norm_2")):
                net.load_param(("dsa_gain", l, j), self.dsa_gain[:, j, :], row_broadcast(ins[name][l], HD),
                               [("x", x0 + 3 * l, 1)], topic="loaded_dsa_gain")
            w = ins["w_in_2"][l]
            st["b_in"] = net.plan_proj(f"dsa{l}_in", w[:, N_A:N_A + N_B], blocks(N_B), KT)
            st["a_in"] = net.plan_proj(f"rwkv{l}_in", w[:, 0:N_A], blocks(N_A), KT)
            net.load_param(("mu", l), self.mu, row_broadcast(ins["rwkv_mu_2"][l], N_A), [(f"dsa{l}", "oT", 1)])
            names = ["rwkv_w0_2", "rwkv_a0_2", "rwkv_kk_2", "rwkv_ka_2", "rwkv_rk_2", "rwkv_v0_2", "rwkv_lnx_g_2", "rwkv_lnx_b_2"]
            for j, name in enumerate(names):
                if name == "rwkv_v0_2":
                    if l == 0:
                        continue
                    src = row_broadcast(ins[name][0], 512)
                else:
                    src = row_broadcast(ins[name][l], 512)
                net.load_param(("vec", l, j), self.vec[:, j, :], src, [("mixed", l)], topic="loaded_rwkv_vectors")
            small = [(slice(0, 64), 0, 512, ins["rwkv_w2_2"][l]), (slice(64, P), 0, 512, ins["rwkv_a2_2"][l]),
                     (slice(0, P), 512, 512, ins["rwkv_g2_2"][l])]
            if l:
                small += [(slice(0, P), 1024, 128, ins["rwkv_v1_2"][0].rearrange("(k p) n -> p k n", p=P)),
                          (slice(0, 32), 1152, 512, ins["rwkv_v2_2"][0])]
            net.piece(("rwkv_small", l), small, 1, SLOT)
            st["merge"] = []
            for nb in range(2):
                c0 = nb * BANK
                st["merge"].append((
                    net.plan_proj(f"gate{l}a{nb}", w[:, N_A + N_B + c0:N_A + N_B + c0 + BANK], [(0, BANK)], KT),
                    net.plan_proj(f"gate{l}b{nb}", w[:, N_A + N_B + D + c0:N_A + N_B + D + c0 + BANK], [(0, BANK)], KT),
                    net.plan_proj(f"branch{l}a{nb}", ins["w_branch_a_2"][l][:, c0:c0 + BANK], [(0, BANK)], 4),
                    net.plan_proj(f"branch{l}b{nb}", ins["w_branch_b_2"][l][:, c0:c0 + BANK], [(0, BANK)], 4)))
            st["out"] = net.plan_proj(f"out{l}", ins["w_out_2"][l], blocks(D), KT)
            net.load_param(("mem_tok", l), self.mem_tok, ins["mem_2"].rearrange("b (m p) n -> p (b m) n", p=P),
                           [(("mergedT", l), m, kg) for m in range(MT) for kg in (0, 4)] + [("groups_done", l)])
            for j, name in enumerate(("mem_q_norm_2", "mem_k_norm_2")):
                net.load_param(("mem_gain", l, j), self.mem_gain[:, j, :], row_broadcast(ins[name][l], P),
                               [("groups_done", l)], topic="loaded_mem_gain")
            st["mkv"] = net.plan_proj(f"mems{l}_kv", ins["mem_wkv_2"][l], blocks(D), KT)
            st["mq"] = net.plan_proj(f"mems{l}_q", ins["mem_wq_2"][l], blocks(512), KT)
            st["mo"] = net.plan_proj(f"mems{l}_o", ins["mem_wo_2"][l], blocks(D), 4)
            if l == 0:
                wg, wu, wd = ins["ffn_wg_2"][0], ins["ffn_wu_2"][0], ins["ffn_wd_2"][0]
                cols = blocks(D_FF)
                st["ffn"] = plan_ffn(net, "ffn_dense", lambda c: (
                    wg[:, cols[c][0]:sum(cols[c])], wu[:, cols[c][0]:sum(cols[c])], wd[cols[c][0]:sum(cols[c]), :]),
                    [cn for _, cn in cols])
            else:
                net.load_param(("router_bias", 0), self.router_bias, row_broadcast(ins["moe_bias_2"], N_EXPERTS))
                net.piece("router", [(slice(0, P), 0, 64, ins["moe_router_2"][0].rearrange("(k p) n -> p k n", p=P))], 1, 64, split=True)
                wg, wu, wd = ins["moe_wg_2"][0], ins["moe_wu_2"][0], ins["moe_wd_2"][0]
                cols = blocks(EXPERT_DIM)
                each = [(e, c0, cn) for e in range(N_EXPERTS) for c0, cn in cols]
                self.each = each
                st["ffn"] = plan_ffn(net, "moe", lambda c: (
                    wg[each[c][0]][:, each[c][1]:each[c][1] + each[c][2]],
                    wu[each[c][0]][:, each[c][1]:each[c][1] + each[c][2]],
                    wd[each[c][0]][each[c][1]:each[c][1] + each[c][2], :]), [cn for _, _, cn in each])
            self.layers.append(st)

    def load_rows(self, name, j, src, after):
        self.net.load_param(name, self.net.norm_buf[:, j * D:(j + 1) * D], row_broadcast(src, D), after)


    def rms_scalar(self, act, tag, src, dst, need):
        for m in range(MT):
            act.wait_ge(*act.at(*need(m)))
            act.raw.activation(dst[:, m, :], src[:, m, :], ACT.Square, accum_out=self.sq[:, m:m + 1]).then_inc(*act.mark("rows_squared", ("squared", tag, m)))

    def rms_vector(self, v, tag, src, dst, j):
        gain = self.net.norm_buf[:, j * D:(j + 1) * D]
        for m in range(MT):
            v.wait_ge(*v.at(("squared", tag, m)))
            v.raw.tensor_scalar(self.sq[:, m:m + 1], self.sq[:, m:m + 1], 1.0 / D, NORM_EPS, ALU.mult, ALU.add).then_inc(*v.mark("variance_ready", ("var", (tag, m))))
            v.wait_ge(*v.at(("rstd", (tag, m)), ("loaded", tag)))
            v.raw.scalar_tensor_tensor(out=dst[:, m, :], in0=src[:, m, :], scalar=self.row_rstd[:, m:m + 1],
                                              in1=gain, op0=ALU.mult, op1=ALU.mult).then_inc(*v.mark("rows_normed", ("hn", tag, m)))

    def rms_gpsimd(self, pool, tag):
        for m in range(MT):
            self.net.rstd_gpsimd(pool, (tag, m), self.sq[:, m:m + 1], self.row_rstd[:, m:m + 1])

    def norm_turn(self, tag, src, dst):
        return self.net.turn_rows(("hT",) + tag, lambda m: src[:, m, :], KT, dst, lambda m: [("hn", tag, m)])

    def turn_need(self, tag):
        return [[(("hT",) + tag, m, kg) for kg in (0, 4)] for m in range(MT)]


    def heads_vector(self, v, tag, x, tmp, gain_parts, at=0, done=("heads_normed",)):
        heads, d = x.shape[2], x.shape[3]
        n = MT * heads
        ss, rs = self.hs[:, at:at + n], self.hr[:, at:at + n]
        sq = tmp.rearrange("p m (h d) -> p m h d", d=d)
        v.raw.tensor_tensor(sq, x, x, ALU.mult).then_inc(*v.step())
        v.wait_ge(*v.last)
        v.raw.tensor_reduce(ss, sq.rearrange("p m h d -> p (m h) d"), AX, ALU.add).then_inc(*v.step())
        v.wait_ge(*v.last)
        v.raw.tensor_scalar(ss, ss, 1.0 / d, NORM_EPS, ALU.mult, ALU.add).then_inc(*v.mark("variance_ready", ("var", tag)))
        v.wait_ge(*v.at(("rstd", tag)))
        for m in range(MT):
            inst = v.raw.tensor_tensor(x[:, m], x[:, m], widen(rs[:, m * heads:(m + 1) * heads], 2, d), ALU.mult)
        inst.then_inc(*v.step())
        v.wait_ge(*v.last)
        for m in range(MT):
            for h0, h1, gain in gain_parts:
                inst = v.raw.tensor_tensor(x[:, m, h0:h1, :], x[:, m, h0:h1, :], widen(gain, 1, h1 - h0), ALU.mult)
        inst.then_inc(*v.mark(*done))
        v.wait_ge(*v.last)


    def angles_vector(self, v):
        v.wait_ge(*v.at(("loaded", ("positions", 1)), ("loaded", ("const", 0))))
        inv = self.net.const("inv_freq")
        magic = float(np.float32(1.5 * 2 ** 23))
        v.raw.tensor_copy(self.pos, self.pos_i.bitcast(I32)).then_inc(*v.step())
        v.wait_ge(*v.last)
        for m in range(MT):
            inst = v.raw.tensor_scalar(self.angle[:, m, :], inv, self.pos[:, m:m + 1], None, ALU.mult)
        inst.then_inc(*v.step())
        v.wait_ge(*v.last)
        v.raw.tensor_scalar(self.turns, self.angle, 1.0 / (2 * np.pi), magic, ALU.mult, ALU.add).then_inc(*v.step())
        v.wait_ge(*v.last)
        v.raw.tensor_scalar(self.turns, self.turns, magic, None, ALU.subtract).then_inc(*v.step())
        v.wait_ge(*v.last)
        c1 = float(np.floor(2 * np.pi * 2 ** 7) / 2 ** 7)
        c2 = float(np.floor((2 * np.pi - c1) * 2 ** 19) / 2 ** 19)
        c3 = 2 * np.pi - c1 - c2
        for c in (c1, c2, c3):
            v.raw.scalar_tensor_tensor(out=self.angle, in0=self.turns, scalar=-c, in1=self.angle, op0=ALU.mult, op1=ALU.add).then_inc(*v.step())
            v.wait_ge(*v.last)
        pi = 3.1415925
        v.raw.tensor_scalar(self.angle, self.angle, pi, -pi, ALU.min, ALU.max).then_inc(*v.step())
        v.wait_ge(*v.last)
        v.raw.tensor_scalar(self.turns, self.angle, float(np.pi / 2), -2 * np.pi, ALU.is_gt, ALU.mult).then_inc(*v.step())
        v.wait_ge(*v.last)
        v.raw.scalar_tensor_tensor(out=self.turns, in0=self.angle, scalar=float(np.pi / 2), in1=self.turns,
                                          op0=ALU.add, op1=ALU.add).then_inc(*v.step())
        v.wait_ge(*v.last)
        v.raw.tensor_scalar(self.turns, self.turns, pi, -pi, ALU.min, ALU.max).then_inc(*v.mark("angles_ready", ("angles", 0)))

    def angles_scalar(self, act):
        act.wait_ge(*act.at(("angles", 0)))
        act.raw.activation(self.sin, self.angle, ACT.Sin)
        act.raw.activation(self.cos, self.turns, ACT.Sin).then_inc(*act.mark("angles_turned", ("tables", 0)))


    def dsa_turn(self, l):
        net, groups = self.net, []
        for which, base in enumerate((0, 640)):
            for m in range(MT):
                groups.append(dict(name=("dsaT", l, which, m), need=[("dsa_ready", l)], bank=2 * which + m,
                                   blocks=[self.colsB[:, m, base + t * P:base + (t + 1) * P] for t in range(4)],
                                   dst=net.qT[:, 4 * which:4 * which + 4, m * P:(m + 1) * P],
                                   by="scalar" if m else "vector"))
        groups.append(dict(name=("dsaT", l, "k"), need=[("dsa_ready", l)], bank=0,
                           blocks=[self.kdup[:, m, w, :] for w in range(2) for m in range(MT)],
                           dst=net.kT[:, 0:2, :].rearrange("p w (m t) -> p (w m) t", m=MT), by="scalar"))
        return groups

    def dsa_heads(self, l):
        net, out = self.net, []
        for h in range(8):
            rows = slice(64 * (h % 2), 64 * (h % 2) + 64)
            out.append(head(
                q=lambda j, m, rows=rows, h=h: net.qT[rows, h // 2, m * P:(m + 1) * P],
                k=lambda j, rows=rows: net.kT[rows, 0, :],
                v=lambda part, kt: self.colsB[:, kt, 576:640],
                out=[(64 * (h % 2), 64, h // 2 % 2)], scale=HD ** -0.5,
                bias=self.chosen, need=[("chosen", l)]))
        return out

    def index_tensor(self, pe, l):
        net = self.net
        pe.wait_ge(*pe.at(*[g["name"] for g in self.dsa_turn(l)]))
        for h in range(8):
            rows = slice(64 * (h % 2), 64 * (h % 2) + 64)
            bank = 4 + h % 4
            pe.wait_ge(*net.free(bank))
            for m in range(MT):
                mm = pe.raw.matmul(net.ps[:, bank, m * S:(m + 1) * S], net.qT[rows, 4 + h // 2, m * P:(m + 1) * P],
                                   net.kT[rows, 1, :], start=True, stop=True)
            mm.then_inc(*net.full(pe, bank, ("index", l, h)))

    def index_scalar(self, act, l):
        net = self.net
        for h in range(8):
            act.wait_ge(*act.at(("index", l, h)))
            if h >= 2:
                act.wait_ge(*act.at(("weighed", l, h - 2)))
            src = net.ps[:, 4 + h % 4, :].rearrange("p (m k) -> p m k", m=MT)
            act.raw.activation(self.relu[:, h % 2], src, ACT.Relu).then_inc(*net.drained(act, 4 + h % 4, ("index", l, h), ("relu", l, h)))

    def index_vector(self, v, l):
        net = self.net
        for h in range(8):
            v.wait_ge(*v.at(("relu", l, h)))
            for m in range(MT):
                w = self.w_idx[:, m, h:h + 1]
                if h == 0:
                    inst = v.raw.tensor_scalar(self.score[:, m, :], self.relu[:, h % 2, m, :], w, None, ALU.mult)
                else:
                    inst = v.raw.scalar_tensor_tensor(out=self.score[:, m, :], in0=self.relu[:, h % 2, m, :], scalar=w,
                                                      in1=self.score[:, m, :], op0=ALU.mult, op1=ALU.add)
            inst.then_inc(*v.mark("index_weighed", ("weighed", l, h)))
            v.wait_ge(*v.last)
        v.raw.tensor_tensor(self.work, self.score, net.const("admissible", MT, S), ALU.add).then_inc(*v.step())
        v.wait_ge(*v.last)
        for m in range(MT):
            for _ in range(S // 4 // 8):
                v.raw.max(self.top8, self.work[:, m, :]).then_inc(*v.step())
                v.wait_ge(*v.last)
                v.raw.match_replace(out=self.work[:, m, :], in_to_replace=self.top8, in_values=self.work[:, m, :],
                                           imm_value=TAKEN).then_inc(*v.step())
                v.wait_ge(*v.last)
        v.raw.tensor_scalar(self.chosen, self.work, -2e38, 1.0, ALU.is_le, ALU.subtract).then_inc(*v.step())
        v.wait_ge(*v.last)
        v.raw.tensor_scalar(self.chosen, self.chosen, -NEG, None, ALU.mult).then_inc(*v.mark("keys_chosen", ("chosen", l)))
        v.wait_ge(*v.last)

    def dsa_prepare_vector(self, v, l):
        net = self.net
        v.wait_ge(*v.at(*net.proj_names(self.layers[l]["b_in"]), *[("loaded", ("dsa_gain", l, j)) for j in range(3)]))
        x = self.colsB[:, :, 0:576].rearrange("p m (h d) -> p m h d", d=HD)
        i = self.colsB[:, :, 640:1216].rearrange("p m (h d) -> p m h d", d=HD)
        tmp = net.part(8192, MT, 576)
        self.heads_vector(v, ("dsa", l), x, tmp, [(0, 8, self.dsa_gain[:, 0, :]), (8, 9, self.dsa_gain[:, 1, :])])
        self.heads_vector(v, ("dsai", l), i[:, :, 8:9, :], tmp[:, :, 0:64], [(0, 1, self.dsa_gain[:, 2, :])], at=20)
        v.wait_ge(*v.at(("tables", 0)))
        temps = [t.rearrange("p m (h d) -> p m h d", d=32) for t in (self.ropeA, self.ropeB)]
        rope(v, v.raw, x, self.cos, self.sin, temps, ("heads_turned", ("dsa_rope", l, 0)))
        v.wait_ge(*v.at(("dsa_rope", l, 0)))
        rope(v, v.raw, i, self.cos, self.sin, temps, ("heads_turned", ("dsa_rope", l, 1)))
        v.wait_ge(*v.at(("dsa_rope", l, 1)))
        for m in range(MT):
            for w, src in enumerate((x[:, m, 8, :], i[:, m, 8, :])):
                v.raw.tensor_copy(self.kdup[:, m, w, :].rearrange("p (e d) -> p e d", e=2), widen(src, 1, 2))
        v.raw.tensor_scalar(self.w_idx, self.colsB[:, :, 1216:1224], HD ** -0.5, 8 ** -0.5, ALU.mult, ALU.mult).then_inc(*v.mark("heads_ready", ("dsa_ready", l)))
        v.wait_ge(*v.last)


    def shift_scalar(self, act, l):
        net = self.net
        act.wait_ge(*act.at(*net.proj_names(self.layers[l]["a_in"]), (f"dsa{l}", "oT", 1), ("zero_row", l)))
        A, B = self.colsA, self.colsS
        act.raw.dma_start(B[1:P, :, :], A[0:P - 1, :, :]).then_inc(*act.mark("rows_shifted", ("shift", l, 0), by=16))
        act.raw.dma_start(B[0:1, 1, :], A[P - 1:P, 0, :]).then_inc(*act.mark("rows_shifted", ("shift", l, 1), by=16))

    def mix_vector(self, v, l):
        A, B = self.colsA, self.colsS
        v.wait_ge(*v.at(("shift", l, 1), ("loaded", ("mu", l))))
        v.raw.tensor_tensor(B, B, A, ALU.subtract).then_inc(*v.step())
        v.wait_ge(*v.last)
        v.raw.tensor_tensor(B, B, widen(self.mu, 1, MT), ALU.mult).then_inc(*v.step())
        v.wait_ge(*v.last)
        v.raw.tensor_tensor(A, A, B, ALU.add).then_inc(*v.mark("columns_mixed", ("mixed", l)))
        v.wait_ge(*v.last)

    def low_rank_turn(self, l):
        g = [dict(name=("low", l, 0), need=[("activated", l)], bank=0,
                  blocks=[self.colsA[:, m, 1536:1664] for m in range(MT)],
                  dst=self.wadT.rearrange("p (m t) -> p m t", m=MT), by="vector"),
             dict(name=("low", l, 1), need=[("activated", l)], bank=1,
                  blocks=[self.colsA[:, m, 1664:1792] for m in range(MT)],
                  dst=self.gdT.rearrange("p (m t) -> p m t", m=MT), by="scalar")]
        if l:
            g += [dict(name=("vT", l, m), need=[("mixed", l)], bank=2 + m,
                       blocks=[self.colsA[:, m, D + t * P:D + (t + 1) * P] for t in range(4)],
                       dst=self.vT[:, :, m * P:(m + 1) * P], by="vector") for m in range(MT)]
        return g

    def low_rank_tensor(self, pe, l):
        net = self.net
        net.turn_tensor(pe, self.low_rank_turn(l))
        w = net.weights(pe, ("rwkv_small", l))[:, 0, :]
        pe.wait_ge(*pe.at(("low", l, 0), ("low", l, 1)))
        for j, (rows, at) in enumerate((((0, 64), 0), ((64, P), 0), ((0, P), 512))):
            src = self.gdT if j == 2 else self.wadT
            for m in range(MT):
                bank = 2 * j + m
                pe.wait_ge(*net.free(bank))
                mm = pe.raw.matmul(net.ps[:, bank, :], src[rows[0]:rows[1], m * P:(m + 1) * P],
                                   w[rows[0]:rows[1], at:at + 512], start=True, stop=True)
                used = [("used", ("rwkv_small", l))] if l == 0 and j == 2 and m == 1 else []
                mm.then_inc(*net.full(pe, bank, ("wag", l, j, m), *used))
        if l:
            pe.wait_ge(*pe.at(*[("vT", l, m) for m in range(MT)]))
            pe.wait_ge(*net.free(6))
            for k in range(4):
                mm = pe.raw.matmul(net.ps[0:32, 6, 0:S], w[:, 1024 + 32 * k:1056 + 32 * k], self.vT[:, k, :],
                                   start=(k == 0), stop=(k == 3))
            mm.then_inc(*net.full(pe, 6, ("vv1", l)))
            pe.wait_ge(*pe.at(("vv", l)))
            for m in range(MT):
                bank = 6 + m
                pe.wait_ge(*net.free(bank))
                mm = pe.raw.matmul(net.ps[:, bank, :], self.vv[0:32, m * P:(m + 1) * P], w[0:32, 1152:1664],
                                   start=True, stop=True)
                used = [("used", ("rwkv_small", l))] if m == 1 else []
                mm.then_inc(*net.full(pe, bank, ("vv2", l, m), *used))

    def prepare_scalar(self, act, l):
        net = self.net
        act.wait_ge(*act.at(("mixed", l)))
        act.raw.activation(self.colsA[:, :, 1536:1600], self.colsA[:, :, 1536:1600], ACT.Tanh)
        act.raw.activation(self.colsA[:, :, 1664:1792], self.colsA[:, :, 1664:1792], ACT.Sigmoid).then_inc(*act.mark("low_rank_activated", ("activated", l)))
        net.turn_copy(act, self.low_rank_turn(l))
        act.wait_ge(*act.at(("wa_biased", l)))
        act.raw.activation(self.sig, self.sig, ACT.Sigmoid).then_inc(*act.mark("decay_sigmoid", ("sig", l)))
        act.raw.activation(self.a, self.a, ACT.Sigmoid).then_inc(*act.mark("rate_sigmoid", ("a", l)))
        for m in range(MT):
            act.wait_ge(*act.at(("wag", l, 2, m)))
            act.raw.activation(self.g[:, m, :], net.ps[:, 4 + m, :], ACT.Copy).then_inc(*net.drained(act, 4 + m, ("wag", l, 2, m), ("g", l, m)))
        if l:
            act.wait_ge(*act.at(("v_biased", l)))
            act.raw.activation(self.tmp, self.tmp, ACT.Sigmoid).then_inc(*act.mark("value_mix_sigmoid", ("vmix", l)))
        for m in range(MT):
            act.wait_ge(*act.at(("cum", l, m)))
            act.raw.activation(self.decay[:, m, :], net.ps[:, m, :], ACT.Exp, scale=-DECAY)
            act.raw.activation(self.undecay[:, m, :], net.ps[:, m, :], ACT.Exp, scale=DECAY).then_inc(*act.mark("decays_ready", ("decays", l, m)))
        act.wait_ge(*act.at(("ends", l)))
        act.raw.activation(self.decay_end, net.ps[:, 2, 0:16].rearrange("p (a c) -> p a c", a=4), ACT.Exp, scale=-DECAY).then_inc(*net.drained(act, 2, ("ends", l), ("decay_end", l)))
        act.wait_ge(*act.at(("before", l)))
        act.raw.activation(self.tmp, self.tmp, ACT.Exp, scale=-DECAY).then_inc(*act.mark("decay_before", ("decay_before", l)))

    def cumulate_tensor(self, pe, l):
        net = self.net
        pe.wait_ge(*pe.at(("sig", l)))
        upto = net.const("upto")
        for m in range(MT):
            pe.wait_ge(*net.free(m))
            pe.raw.matmul(net.ps[:, m, :], upto, self.sig[:, m, :], start=True, stop=True).then_inc(*net.full(pe, m, ("cum", l, m)))
        pe.wait_ge(*net.free(2))
        for pair in range(4):
            for m in range(MT):
                mm = pe.raw.matmul(net.ps[:, 2, 4 * pair + 2 * m:4 * pair + 2 * m + 2], self.sig[:, m, pair * P:(pair + 1) * P],
                                   upto[:, CH - 1:P:CH], start=True, stop=True)
        mm.then_inc(*net.full(pe, 2, ("ends", l)))

    def prepare_vector(self, v, l):
        net, vec = self.net, self.vec
        row = lambda j: widen(vec[:, j, :], 1, MT)
        net.turn_copy(v, self.low_rank_turn(l))
        v.wait_ge(*v.at(("loaded", ("vec", l, 7))))
        for j, dst in ((0, self.sig), (1, self.a)):
            for m in range(MT):
                v.wait_ge(*v.at(("wag", l, j, m)))
                v.raw.tensor_tensor(dst[:, m, :], net.ps[:, 2 * j + m, :], vec[:, j, :], ALU.add).then_inc(*net.drained(v, 2 * j + m, ("wag", l, j, m), ("wa_biased", l) if (j, m) == (1, 1) else ("wab", l, j, m)))
        if l:
            v.wait_ge(*v.at(("vv1", l)))
            v.raw.tensor_copy(self.vv[0:32, :], net.ps[0:32, 6, 0:S]).then_inc(*net.drained(v, 6, ("vv1", l), ("vv", l)))
            for m in range(MT):
                v.wait_ge(*v.at(("vv2", l, m)))
                v.raw.tensor_tensor(self.tmp[:, m, :], net.ps[:, 6 + m, :], vec[:, 5, :], ALU.add).then_inc(*net.drained(v, 6 + m, ("vv2", l, m), ("v_biased", l) if m else ("vb", l)))
        x = lambda ap: ap.rearrange("p m (h d) -> p m h d", d=HD)
        v.raw.tensor_tensor(self.kk, self.k, row(2), ALU.mult).then_inc(*v.step())
        v.wait_ge(*v.last)
        v.raw.tensor_tensor(self.at, self.kk, self.kk, ALU.mult).then_inc(*v.step())
        v.wait_ge(*v.last)
        v.raw.tensor_reduce(self.hs[:, 0:16], self.at.rearrange("p m (h d) -> p (m h) d", d=HD), AX, ALU.add).then_inc(*v.step())
        v.wait_ge(*v.last)
        v.raw.tensor_scalar(self.hs[:, 0:16], self.hs[:, 0:16], 1e-24, None, ALU.max).then_inc(*v.mark("variance_ready", ("var", ("kk", l))))
        v.wait_ge(*v.at(("a", l)))
        v.raw.scalar_tensor_tensor(out=self.bh, in0=self.a, scalar=1.0, in1=row(3), op0=ALU.subtract, op1=ALU.mult).then_inc(*v.step())
        v.wait_ge(*v.last)
        v.raw.scalar_tensor_tensor(out=self.k, in0=self.bh, scalar=1.0, in1=self.k, op0=ALU.add, op1=ALU.mult).then_inc(*v.step())
        v.wait_ge(*v.last)
        v.raw.tensor_tensor(self.bh, self.r, self.k, ALU.mult).then_inc(*v.step())
        v.wait_ge(*v.last)
        v.raw.tensor_tensor(self.bh, self.bh, row(4), ALU.mult).then_inc(*v.step())
        v.wait_ge(*v.last)
        v.raw.tensor_reduce(self.bonus.rearrange("p m h -> p (m h)"), self.bh.rearrange("p m (h d) -> p (m h) d", d=HD),
                                   AX, ALU.add).then_inc(*v.step())
        v.wait_ge(*v.last)
        if l:
            v.wait_ge(*v.at(("vmix", l)))
            v.raw.tensor_tensor(self.bh, net.vfirst[:, :].rearrange("p (m n) -> p m n", m=MT), self.v, ALU.subtract).then_inc(*v.step())
            v.wait_ge(*v.last)
            v.raw.tensor_tensor(self.bh, self.bh, self.tmp, ALU.mult).then_inc(*v.step())
            v.wait_ge(*v.last)
            v.raw.tensor_tensor(self.v, self.v, self.bh, ALU.add).then_inc(*v.step())
            v.wait_ge(*v.last)
        else:
            v.raw.tensor_copy(net.vfirst[:, :].rearrange("p (m n) -> p m n", m=MT), self.v).then_inc(*v.step())
            v.wait_ge(*v.last)
        for m in range(MT):
            v.wait_ge(*v.at(("cum", l, m)))
            v.wait_ge(*v.at(("decays", l, m)))
            v.raw.tensor_tensor(self.tmp[:, m, :], net.ps[:, m, :], self.sig[:, m, :], ALU.subtract).then_inc(*net.drained(v, m, ("cum", l, m), ("before", l) if m else ("before0", l)))
        v.wait_ge(*v.at(("rstd", ("kk", l))))
        for m in range(MT):
            inst = v.raw.tensor_tensor(x(self.kk)[:, m], x(self.kk)[:, m], widen(self.hr[:, 8 * m:8 * m + 8], 2, HD), ALU.mult)
        inst.then_inc(*v.step())
        v.wait_ge(*v.last)
        v.raw.tensor_tensor(self.bh, self.kk, self.a, ALU.mult).then_inc(*v.step())
        v.wait_ge(*v.last)
        v.raw.tensor_tensor(self.bh, self.bh, self.undecay, ALU.mult).then_inc(*v.mark("operand_b", ("bh", l)))
        v.wait_ge(*v.last)
        v.raw.tensor_tensor(self.k, self.k, self.undecay, ALU.mult).then_inc(*v.mark("operand_k", ("kh", l)))
        v.wait_ge(*v.last)
        v.raw.tensor_tensor(self.r, self.r, self.decay, ALU.mult).then_inc(*v.mark("operand_r", ("rt", l)))
        v.wait_ge(*v.last)
        v.wait_ge(*v.at(("decay_before", l)))
        v.raw.scalar_tensor_tensor(out=self.at, in0=self.kk, scalar=-1.0, in1=self.tmp, op0=ALU.mult, op1=ALU.mult).then_inc(*v.mark("operand_a", ("at", l)))
        v.wait_ge(*v.last)

    def operand_turn(self, l):
        net, groups = self.net, []
        i = 0
        need = [(n, l) for n in ("at", "rt", "bh", "kh")]
        for which, (src, name) in enumerate(((self.at, "a"), (self.r, "r"), (self.bh, "b"), (self.k, "k"))):
            for m in range(MT):
                if which < 2:
                    dst = self.arT[:, :, m, which * P:(which + 1) * P]
                else:
                    dst = (self.bT if which == 2 else self.khT)[:, :, m * P:(m + 1) * P]
                groups.append(dict(name=("operand", l, name, m), need=need, bank=i % 8,
                                   blocks=[src[:, m, t * P:(t + 1) * P] for t in range(4)], dst=dst,
                                   by="scalar" if i % 2 else "vector"))
                i += 1
        return groups


    def group_banks(self, par):
        return ((2, 4, 5), (3, 6, 7))[par]

    def solve_tensor(self, pe, l):
        net = self.net
        pe.wait_ge(*pe.at(*[g["name"] for g in self.operand_turn(l)]))
        for duo in range(2):
            for i in range(8):
                n = 8 * duo + i
                m, h = divmod(n, 8)
                rows = slice(64 * (h % 2), 64 * (h % 2) + 64)
                bank = i % 2
                pe.wait_ge(*net.free(bank))
                for which, src in enumerate((self.bT, self.khT)):
                    mm = pe.raw.matmul(net.ps[:, bank, which * S:(which + 1) * S], src[rows, h // 2, m * P:(m + 1) * P],
                                       self.arT[rows, h // 2, m, :], start=True, stop=True)
                mm.then_inc(*net.full(pe, bank, ("pairs", l, n)))
            for lev in range(6):
                for par in range(2):
                    bw, bx, by = self.group_banks(par)
                    key = (l, duo, par, lev)
                    if lev == 0:
                        pe.wait_ge(*pe.at(("LT", l, 8 * duo + 4 * par + 3)))
                    else:
                        pe.wait_ge(*pe.at(("XY", l, duo, par, lev - 1)))
                    pe.wait_ge(*net.free(bw))
                    for q in range(4):
                        X = net.ident if lev == 0 else self.X[par][:, q, :]
                        mm = pe.raw.matmul(net.ps[:, bw, q * P:(q + 1) * P], self.LT[par][:, q, :], X, start=True, stop=True)
                    mm.then_inc(*net.full(pe, bw, ("W", *key)))
                for par in range(2):
                    bw, bx, by = self.group_banks(par)
                    key = (l, duo, par, lev)
                    pe.wait_ge(*pe.at(("Wm", *key)))
                    for bank, name in ((bx, "dX"), (by, "dY")):
                        if name == "dX" and lev == 5:
                            continue
                        pe.wait_ge(*net.free(bank))
                        for q in range(4):
                            Y = net.ident if lev == 0 else self.Y[par][:, q, :]
                            W = self.W[par][:, q, :]
                            mm = pe.raw.matmul(net.ps[:, bank, q * P:(q + 1) * P], *((Y, W) if name == "dX" else (W, Y)),
                                               start=True, stop=True)
                        mm.then_inc(*net.full(pe, bank, (name, *key)))

    def solve_vector(self, v, l):
        net = self.net
        before = net.const("before")
        for duo in range(2):
            for i in range(8):
                n = 8 * duo + i
                bank = i % 2
                v.wait_ge(*v.at(("pairs", l, n)))
                if duo and i % 4 == 0:
                    v.wait_ge(*v.at(("solved", l, 2 * (duo - 1) + i // 4)))
                v.raw.tensor_tensor(self.LT[i // 4][:, i % 4, :], net.ps[:, bank, 0:P], before, ALU.mult)
                for half in range(2):
                    rows = slice(64 * half, 64 * half + 64)
                    src = net.ps[rows, bank, P:4 * P].rearrange("p (a t) -> p a t", a=3)[:, :, 64 * half:64 * half + 64]
                    inst = v.raw.tensor_tensor(self.packed[rows, n], src,
                                               net.const("packed", 3, CH)[rows], ALU.mult)
                inst.then_inc(*net.drained(v, bank, ("pairs", l, n), ("LT", l, n)))
            for lev in range(6):
                for par in range(2):
                    bw = self.group_banks(par)[0]
                    key = (l, duo, par, lev)
                    v.wait_ge(*v.at(("W", *key)))
                    src = net.ps[:, bw, :].rearrange("p (q t) -> p q t", q=4)
                    v.raw.tensor_tensor(self.W[par], src, widen(net.const(f"level{2 ** lev}"), 1, 4), ALU.mult).then_inc(*net.drained(v, bw, ("W", *key), ("Wm", *key)))
                for par in range(2):
                    bw, bx, by = self.group_banks(par)
                    key = (l, duo, par, lev)
                    if lev < 5:
                        v.wait_ge(*v.at(("dX", *key)))
                        X = widen(net.ident, 1, 4) if lev == 0 else self.X[par]
                        v.raw.tensor_tensor(self.X[par], net.ps[:, bx, :].rearrange("p (q t) -> p q t", q=4), X, ALU.add).then_inc(*net.drained(v, bx, ("dX", *key)))
                    v.wait_ge(*v.at(("dY", *key)))
                    Y = widen(net.ident, 1, 4) if lev == 0 else self.Y[par]
                    v.raw.tensor_tensor(self.Y[par], net.ps[:, by, :].rearrange("p (q t) -> p q t", q=4), Y, ALU.add).then_inc(*net.drained(v, by, ("dY", *key), ("XY", *key)))

    def solve_scalar(self, act, l):
        for duo in range(2):
            for par in range(2):
                act.wait_ge(*act.at(("XY", l, duo, par, 5)))
                n0 = 8 * duo + 4 * par
                for half in range(2):
                    rows = slice(64 * half, 64 * half + 64)
                    inst = act.raw.activation(self.solve[rows, n0:n0 + 4, :], self.Y[par][rows, :, 64 * half:64 * half + 64], ACT.Copy)
                inst.then_inc(*act.mark("inverse_kept", ("solved", l, 2 * duo + par)))

    def zeros_gpsimd(self, pool, l):
        pool.wait_ge(*pool.at(*[("solved", l, i) for i in range(4)]))
        for half in range(2):
            other = slice(64 * (1 - half), 64 * (1 - half) + 64)
            pool.raw.memset(self.rhs[other, half, :], 0.0)
            pool.raw.memset(self.sa[other, half, :], 0.0)
            pool.raw.memset(self.v_half[other, half], 0.0)
            for s in self.state:
                inst = pool.raw.memset(s[other, :, 64 * half:64 * half + 64], 0.0)
        inst.then_inc(*pool.mark("operands_zeroed", ("zeroed", l)))

    def chunks_tensor(self, pe, l):
        net = self.net
        pe.wait_ge(*pe.at(*[("solved", l, i) for i in range(4)], ("zeroed", l), ("v_halves", l)))
        for c in range(4):
            m, half = divmod(c, 2)
            rows = slice(64 * half, 64 * half + 64)
            last, state = c == 3, self.state[c % 2]
            hd = [slice(h * 64, h * 64 + 64) for h in range(8)]
            pair = [slice(i * P, i * P + P) for i in range(4)]
            V, R, SA = self.v_half[:, half, m], self.rhs[:, half], self.sa[:, half]
            if c:
                pe.wait_ge(*pe.at(("state", l, c)))

            def mm(bank, out_rows, at, lhsT, rhs, start, stop=False):
                return pe.raw.matmul(net.ps[out_rows, bank, at], lhsT, rhs, start=start, stop=stop, skip_group_check=True)

            bank = c % 2
            pe.wait_ge(*net.free(bank))
            for h in range(8):
                x = mm(bank, rows, hd[h], self.packed[:, 8 * m + h, 1, :], V[:, hd[h]], h == 0, c == 0)
            if c:
                for i in range(4):
                    x = mm(bank, rows, pair[i], self.arT[:, i, m, rows], state[:, i, :], False, True)
            x.then_inc(*net.full(pe, bank, ("rhs", l, c)))
            by, bs = 4 + c % 2, 6 + c % 2
            pe.wait_ge(*net.free(by))
            for h in range(8):
                mm(by, rows, hd[h], self.packed[:, 8 * m + h, 2, :], V[:, hd[h]], h == 0)
            if c:
                for i in range(4):
                    mm(by, rows, pair[i], self.arT[:, i, m, P + 64 * half:P + 64 * half + 64], state[:, i, :], False)
            if not last:
                pe.wait_ge(*net.free(bs))
                for i in range(4):
                    mm(bs, slice(0, P), pair[i], self.k[:, m, pair[i]], V[:, pair[i]], i == 0)
                    if c:
                        mm(bs, slice(0, P), pair[i], net.ident, state[:, i, :], False)
            pe.wait_ge(*pe.at(("rhs_kept", l, c)))
            bank = 2 + c % 2
            pe.wait_ge(*net.free(bank))
            for h in range(8):
                x = mm(bank, rows, hd[h], self.solve[:, 8 * m + h, :], R[:, hd[h]], h == 0, True)
            x.then_inc(*net.full(pe, bank, ("sa", l, c)))
            pe.wait_ge(*pe.at(("sa_kept", l, c)))
            if not last:
                for i in range(4):
                    x = mm(bs, slice(0, P), pair[i], self.bh[:, m, pair[i]], SA[:, pair[i]], False, True)
                x.then_inc(*net.full(pe, bs, ("new_state", l, c)))
            for h in range(8):
                x = mm(by, rows, hd[h], self.packed[:, 8 * m + h, 0, :], SA[:, hd[h]], False, True)
            x.then_inc(*net.full(pe, by, ("y", l, c)))

    def chunks_scalar(self, act, l):
        net = self.net
        act.wait_ge(*act.at(("solved", l, 3), ("zeroed", l)))
        for half in range(2):
            rows = slice(64 * half, 64 * half + 64)
            inst = act.raw.activation(self.v_half[rows, half], self.v[rows], ACT.Copy)
        inst.then_inc(*act.mark("values_halved", ("v_halves", l)))
        for c in range(4):
            m, half = divmod(c, 2)
            rows = slice(64 * half, 64 * half + 64)
            if c == 0:
                act.wait_ge(*act.at(("zeroed", l)))
            act.wait_ge(*act.at(("sa", l, c)))
            act.raw.activation(self.sa[rows, half, :], net.ps[rows, 2 + c % 2, :], ACT.Copy).then_inc(*net.drained(act, 2 + c % 2, ("sa", l, c), ("sa_kept", l, c)))
            act.wait_ge(*act.at(("y", l, c)))
            act.raw.activation(self.y[rows, m, :], net.ps[rows, 4 + c % 2, :], ACT.Copy).then_inc(*net.drained(act, 4 + c % 2, ("y", l, c), ("y_kept", l, c)))

    def chunks_vector(self, v, l):
        net = self.net
        v.wait_ge(*v.at(("zeroed", l), ("decay_end", l)))
        for c in range(4):
            half = c % 2
            rows = slice(64 * half, 64 * half + 64)
            v.wait_ge(*v.at(("rhs", l, c)))
            v.raw.tensor_copy(self.rhs[rows, half, :], net.ps[rows, c % 2, :]).then_inc(*net.drained(v, c % 2, ("rhs", l, c), ("rhs_kept", l, c)))
            if c < 3:
                v.wait_ge(*v.at(("new_state", l, c)))
                for e in range(2):
                    rows = slice(64 * e, 64 * e + 64)
                    src = net.ps[rows, 6 + c % 2, :].rearrange("p (a d) -> p a d", a=4)[:, :, rows]
                    inst = v.raw.tensor_tensor(self.state[(c + 1) % 2][rows, :, rows], src,
                                               widen(self.decay_end[rows, :, c], 2, CH), ALU.mult)
                inst.then_inc(*net.drained(v, 6 + c % 2, ("new_state", l, c), ("state", l, c + 1)))

    def finish_vector(self, v, l):
        net = self.net
        flat = lambda ap: ap.rearrange("p m (h d) -> p (m h) d", d=HD)
        by_head = lambda ap, at: ap[:, at:at + 16]
        tmp = self.at
        v.wait_ge(*v.at(*[("y_kept", l, c) for c in range(4)], ("g", l, 1)))
        v.raw.tensor_reduce(by_head(self.hs, 0), flat(self.y), AX, ALU.add).then_inc(*v.step())
        v.wait_ge(*v.last)
        v.raw.tensor_scalar(by_head(self.hs, 0), by_head(self.hs, 0), 1.0 / HD, None, ALU.mult).then_inc(*v.step())
        v.wait_ge(*v.last)
        v.raw.tensor_tensor(flat(self.y), flat(self.y), widen(by_head(self.hs, 0), 2, HD), ALU.subtract).then_inc(*v.step())
        v.wait_ge(*v.last)
        v.raw.tensor_tensor(tmp, self.y, self.y, ALU.mult).then_inc(*v.step())
        v.wait_ge(*v.last)
        v.raw.tensor_reduce(by_head(self.hs, 16), flat(tmp), AX, ALU.add).then_inc(*v.step())
        v.wait_ge(*v.last)
        v.raw.tensor_scalar(by_head(self.hs, 16), by_head(self.hs, 16), 1.0 / HD, LNX_EPS, ALU.mult, ALU.add).then_inc(*v.mark("variance_ready", ("var", ("lnx", l))))
        bonus = self.bonus
        for m in range(MT):
            inst = v.raw.tensor_tensor(tmp[:, m, :].rearrange("p (h d) -> p h d", d=HD),
                                       self.v[:, m, :].rearrange("p (h d) -> p h d", d=HD), widen(bonus[:, m, :], 2, HD), ALU.mult)
        inst.then_inc(*v.step())
        v.wait_ge(*v.last)
        v.wait_ge(*v.at(("rstd", ("lnx", l))))
        v.raw.tensor_tensor(flat(self.y), flat(self.y), widen(by_head(self.hr, 16), 2, HD), ALU.mult).then_inc(*v.step())
        v.wait_ge(*v.last)
        v.raw.tensor_tensor(self.y, self.y, widen(self.vec[:, 6, :], 1, MT), ALU.mult).then_inc(*v.step())
        v.wait_ge(*v.last)
        v.raw.tensor_tensor(self.y, self.y, widen(self.vec[:, 7, :], 1, MT), ALU.add).then_inc(*v.step())
        v.wait_ge(*v.last)
        v.raw.tensor_tensor(self.y, self.y, tmp, ALU.add).then_inc(*v.step())
        v.wait_ge(*v.last)
        v.raw.tensor_tensor(self.y, self.y, self.g, ALU.mult).then_inc(*v.mark("rwkv_done", ("ya", l)))
        v.wait_ge(*v.last)

    def ya_turn(self, l):
        return [dict(name=("yaT", l, m), need=[("ya", l)], bank=m,
                     blocks=[self.y[:, m, t * P:(t + 1) * P] for t in range(4)],
                     dst=self.yaT[:, :, m * P:(m + 1) * P], by="scalar" if m else "vector") for m in range(MT)]


    def merge_tensor(self, pe, l):
        net = self.net
        lhs = [lambda k, m: net.xT[:, k, m * P:(m + 1) * P]] * 2 + [
            lambda k, m: self.yaT[:, k, m * P:(m + 1) * P], lambda k, m: self.ybT[:, k, m * P:(m + 1) * P]]
        for nb, prs in enumerate(self.layers[l]["merge"]):
            for j, pr in enumerate(prs):
                need = [[("yaT", l, m)] for m in range(MT)] if j == 2 else ()
                net.proj_tensor(pe, pr, lhs[j], lambda b, m, j=j: 2 * j + m, need)

    def merge_scalar(self, act, l):
        net = self.net
        act.wait_ge(*act.at(("ya", l), ("yaT", l, 0), ("yaT", l, 1)))
        for nb, prs in enumerate(self.layers[l]["merge"]):
            for j in range(2):
                for m in range(MT):
                    act.wait_ge(*act.at((prs[j]["tag"], "full", 0, m)))
                    act.raw.activation(self.gate[j][:, m, nb * BANK:(nb + 1) * BANK],
                                                        net.ps[:, 2 * j + m, :], ACT.Sigmoid).then_inc(*net.drained(act, 2 * j + m, (prs[j]["tag"], "full", 0, m), ("gate", l, nb, j, m)))

    def merge_vector(self, v, l):
        net = self.net
        for nb, prs in enumerate(self.layers[l]["merge"]):
            cols = slice(nb * BANK, (nb + 1) * BANK)
            for m in range(MT):
                out = self.merged[:, m, cols]
                v.wait_ge(*v.at((prs[2]["tag"], "full", 0, m), ("gate", l, nb, 0, m)))
                v.raw.tensor_tensor(out, net.ps[:, 4 + m, :], self.gate[0][:, m, cols], ALU.mult).then_inc(*net.drained(v, 4 + m, (prs[2]["tag"], "full", 0, m), ("ga", l, nb, m)))
            for m in range(MT):
                out, gb = self.merged[:, m, cols], self.gate[1][:, m, cols]
                v.wait_ge(*v.at((prs[3]["tag"], "full", 0, m), ("gate", l, nb, 1, m)))
                v.raw.tensor_tensor(gb, net.ps[:, 6 + m, :], gb, ALU.mult).then_inc(*net.drained(v, 6 + m, (prs[3]["tag"], "full", 0, m), ("gb", l, nb, m)))
                v.wait_ge(*v.at(("gb", l, nb, m), ("ga", l, nb, m)))
                v.raw.tensor_tensor(out, out, gb, ALU.add).then_inc(*v.mark("branches_merged", *([("merged", l, m)] if nb == 1 else []), *([("groups_done", l)] if nb == 1 and m == 1 else [])))

    def merged_turn(self, l):
        return self.net.turn_rows(("mergedT", l), lambda m: self.merged[:, m, :], KT, self.mergedT,
                                  lambda m: [("merged", l, m)])

    def add_vector(self, v, n, names):
        net = self.net
        for m in range(MT):
            v.wait_ge(*v.at(*names(m)))
            for nb in range(2):
                cols = slice(nb * BANK, (nb + 1) * BANK)
                inst = v.raw.tensor_tensor(net.x[:, m, cols], net.x[:, m, cols], net.ps[:, 4 + 2 * m + nb, :], ALU.add)
                inst.then_inc(*net.drained(v, 4 + 2 * m + nb, names(m)[nb], *([("x", n + 1, m)] if nb else [])))
            v.wait_ge(*v.last)


    def mem_take(self, b, m):
        net = self.net
        return "scalar", lambda e, ps: net.copy(e, net.v_tok[:, m, b * BANK:(b + 1) * BANK], ps)

    def q_take(self, b, m):
        net = self.net
        return "scalar", lambda e, ps: net.copy(e, self.q_tok[:, m, :], ps)

    def small_turn(self, tag, src, dst):
        return [dict(name=(tag, m), need=[tag], bank=m, blocks=[src[:, m, t * P:(t + 1) * P] for t in range(4)],
                     dst=dst[:, 0:4, m * P:(m + 1) * P], by="scalar" if m else "vector") for m in range(MT)]

    def mem_heads(self):
        net, out = self.net, []
        for h in range(4):
            out.append(head(
                q=lambda j, m, h=h: net.qT[:, h, m * P:(m + 1) * P],
                k=lambda j, h=h: net.kT[:, h, :],
                v=lambda part, kt, h=h: net.v_tok[:, kt, 512 + P * h:512 + P * (h + 1)],
                out=[(0, P, h % 2)], scale=P ** -0.5))
        return out


    def router_tensor(self, pe):
        net = self.net
        w = at_k(net.weights(pe, "router"), 0)
        need = self.turn_need(("ffn", 1))
        pe.wait_ge(*net.free(4))
        for m in range(MT):
            pe.wait_ge(*pe.at(*need[m]))
            for k in range(KT):
                mm = net.product(pe, net.ps[:, 4, 8 * m:8 * m + 8], pick(net.xT_halves, k, m),
                                 tuple(h[:, 8 * k:8 * k + 8] for h in w), k == 0, k == KT - 1)
        mm.then_inc(*net.full(pe, 4, "logits", ("used", "router")))

    def router_vector(self, v):
        net = self.net
        lg, g = self.logits, self.gates
        bias = widen(self.router_bias, 1, MT)
        v.wait_ge(*v.at("logits", ("loaded", ("router_bias", 0))))
        v.raw.tensor_tensor(lg, net.ps[:, 4, 0:16].rearrange("p (m e) -> p m e", m=MT), bias, ALU.add).then_inc(*net.drained(v, 4, "logits", "lg"))
        v.wait_ge(*v.at("lg"))
        tmp = net.part(20480, 8, 8)
        tmp2 = net.part(20544, 8, 8)
        v.raw.tensor_reduce(self.gate_sum, lg, AX, ALU.max).then_inc(*v.step())
        v.wait_ge(*v.last)
        v.raw.tensor_tensor(g, lg, widen(self.gate_sum, 2, 8), ALU.subtract).then_inc(*v.mark("gates_centred", "centred"))
        v.wait_ge(*v.last)
        v.wait_ge(*v.at("gates_exp"))
        for m in range(MT):
            mine, other = widen(lg[:, m, :], 2, 8), widen(lg[:, m, :], 1, 8)
            v.raw.tensor_tensor(tmp, other, mine, ALU.is_equal).then_inc(*v.step())
            v.wait_ge(*v.last)
            v.raw.tensor_tensor(tmp, tmp, net.const("lower_index", 8, 8), ALU.mult).then_inc(*v.step())
            v.wait_ge(*v.last)
            v.raw.tensor_tensor(tmp2, other, mine, ALU.is_gt).then_inc(*v.step())
            v.wait_ge(*v.last)
            v.raw.tensor_tensor(tmp, tmp, tmp2, ALU.add).then_inc(*v.step())
            v.wait_ge(*v.last)
            v.raw.tensor_reduce(self.hs[:, 0:8], tmp, AX, ALU.add).then_inc(*v.step())
            v.wait_ge(*v.last)
            v.raw.tensor_scalar(self.hs[:, 0:8], self.hs[:, 0:8], 1.5, None, ALU.is_lt).then_inc(*v.step())
            v.wait_ge(*v.last)
            v.raw.tensor_tensor(g[:, m, :], g[:, m, :], self.hs[:, 0:8], ALU.mult).then_inc(*v.step())
            v.wait_ge(*v.last)
        v.raw.tensor_reduce(self.gate_sum, g, AX, ALU.add).then_inc(*v.step())
        v.wait_ge(*v.last)
        v.raw.reciprocal(self.gate_sum, self.gate_sum).then_inc(*v.step())
        v.wait_ge(*v.last)
        v.raw.tensor_tensor(g, g, widen(self.gate_sum, 2, 8), ALU.mult).then_inc(*v.step())
        v.wait_ge(*v.last)


    def out_bank(self, b, m):
        return 4 + 2 * m + b

    def tensor(self, pe):
        net = self.net
        rot = lambda b, m: (2 * b + m) % 4
        xT = lambda k, m: net.xT[:, k, m * P:(m + 1) * P]
        for l, st in enumerate(self.layers):
            net.turn_tensor(pe, self.norm_turn(("mix", l), net.ax, net.xT))
            net.proj_tensor(pe, st["b_in"], xT, rot, self.turn_need(("mix", l)))
            net.proj_tensor(pe, st["a_in"], xT, rot)
            net.turn_tensor(pe, self.dsa_turn(l))
            self.index_tensor(pe, l)
            attn_tensor(net, pe, f"dsa{l}", self.dsa_heads(l), 4)
            self.low_rank_tensor(pe, l)
            self.cumulate_tensor(pe, l)
            net.turn_tensor(pe, self.operand_turn(l))
            self.solve_tensor(pe, l)
            self.chunks_tensor(pe, l)
            net.turn_tensor(pe, self.ya_turn(l))
            self.merge_tensor(pe, l)
            net.turn_tensor(pe, self.merged_turn(l))
            turned = [[(("mergedT", l), m, kg) for kg in (0, 4)] for m in range(MT)]
            net.proj_tensor(pe, st["out"], lambda k, m: self.mergedT[:, k, m * P:(m + 1) * P], self.out_bank, turned)
            net.turn_tensor(pe, self.norm_turn(("memt", l), self.mem_tok, self.memT))
            net.proj_tensor(pe, st["mkv"], lambda k, m: self.memT[:, k, m * P:(m + 1) * P], rot, self.turn_need(("memt", l)))
            net.turn_tensor(pe, self.small_turn(("mem_k", l), net.v_tok, net.kT))
            net.turn_tensor(pe, self.norm_turn(("memx", l), net.ax, net.xT))
            net.proj_tensor(pe, st["mq"], xT, rot, self.turn_need(("memx", l)))
            net.turn_tensor(pe, self.small_turn(("mem_q", l), self.q_tok, net.qT))
            attn_tensor(net, pe, f"mems{l}", self.mem_heads(), 2,
                        need_q=[(("mem_q", l), m) for m in range(MT)] + [(("mem_k", l), m) for m in range(MT)])
            done = [(f"mems{l}", "oT", g) for g in range(2)]
            net.proj_tensor(pe, st["mo"], lambda k, m: net.oT[:, k, m * P:(m + 1) * P], self.out_bank, [done, done])
            net.turn_tensor(pe, self.norm_turn(("ffn", l), net.ax, net.xT_halves))
            if l:
                self.router_tensor(pe)
            ffn_tensor(net, pe, st["ffn"], self.turn_need(("ffn", l)))

    def scalar(self, act):
        net = self.net
        self.angles_scalar(act)
        rot = lambda b, m: (2 * b + m) % 4
        for l, st in enumerate(self.layers):
            n = self.x0 + 3 * l
            self.rms_scalar(act, ("mix", l), net.x, net.ax, lambda m: [("x", n, m)])
            net.turn_copy(act, self.norm_turn(("mix", l), net.ax, net.xT))
            copy = lambda dst: lambda b, m: ("scalar", lambda e, ps: net.copy(e, dst[:, m, b * BANK:b * BANK + ps.shape[1]], ps))
            net.proj_copy(act, st["b_in"], rot, copy(self.colsB))
            net.proj_copy(act, st["a_in"], rot, copy(self.colsA))
            net.turn_copy(act, self.dsa_turn(l))
            self.index_scalar(act, l)
            attn_scalar(net, act, f"dsa{l}", self.dsa_heads(l))
            self.shift_scalar(act, l)
            self.prepare_scalar(act, l)
            net.turn_copy(act, self.operand_turn(l))
            self.solve_scalar(act, l)
            self.chunks_scalar(act, l)
            net.turn_copy(act, self.ya_turn(l))
            self.merge_scalar(act, l)
            net.turn_copy(act, self.merged_turn(l))
            self.rms_scalar(act, ("memt", l), self.mem_tok, net.v_tok, lambda m: [("loaded", ("mem_tok", l))])
            net.turn_copy(act, self.norm_turn(("memt", l), self.mem_tok, self.memT))
            net.proj_copy(act, st["mkv"], rot, self.mem_take)
            net.turn_copy(act, self.small_turn(("mem_k", l), net.v_tok, net.kT))
            self.rms_scalar(act, ("memx", l), net.x, net.ax, lambda m: [("x", n + 1, m)])
            net.turn_copy(act, self.norm_turn(("memx", l), net.ax, net.xT))
            net.proj_copy(act, st["mq"], rot, self.q_take)
            net.turn_copy(act, self.small_turn(("mem_q", l), self.q_tok, net.qT))
            attn_scalar(net, act, f"mems{l}", self.mem_heads())
            ahead = (["router"] if l else []) + st["ffn"]["gate_up"][0]
            net.split_scalar(act, ahead[:2])
            self.rms_scalar(act, ("ffn", l), net.x, net.ax, lambda m: [("x", n + 2, m)])
            net.turn_copy(act, self.norm_turn(("ffn", l), net.ax, net.xT_halves))
            net.split_scalar(act, ahead[2:])
            if l:
                act.wait_ge(*act.at("centred"))
                act.raw.activation(self.gates, self.gates, ACT.Exp).then_inc(*act.mark("gates_exponential", "gates_exp"))
            ffn_scalar(net, act, st["ffn"])

    def vector(self, v):
        net = self.net
        self.angles_vector(v)
        for l, st in enumerate(self.layers):
            n = self.x0 + 3 * l
            v.wait_ge(*v.at(("x", n, 0), ("x", n, 1)))
            self.rms_vector(v, ("mix", l), net.x, net.ax, 0)
            net.turn_copy(v, self.norm_turn(("mix", l), net.ax, net.xT))
            self.dsa_prepare_vector(v, l)
            net.turn_copy(v, self.dsa_turn(l))
            self.index_vector(v, l)
            attn_vector(net, v, f"dsa{l}", self.dsa_heads(l), 4)
            v.wait_ge(*v.at((f"dsa{l}", "oT", 1)))
            v.raw.memset(self.colsS[0:1, 0, :], 0.0).then_inc(*v.mark("zero_row_ready", ("zero_row", l)))
            self.mix_vector(v, l)
            self.prepare_vector(v, l)
            net.turn_copy(v, self.operand_turn(l))
            self.solve_vector(v, l)
            self.chunks_vector(v, l)
            self.finish_vector(v, l)
            net.turn_copy(v, self.ya_turn(l))
            self.merge_vector(v, l)
            net.turn_copy(v, self.merged_turn(l))
            self.rms_vector(v, ("memt", l), self.mem_tok, self.mem_tok, 2)
            net.turn_copy(v, self.norm_turn(("memt", l), self.mem_tok, self.memT))
            self.add_vector(v, n, lambda m: [(st["out"]["tag"], "full", b, m) for b in range(2)])
            x4 = lambda ap: ap.rearrange("p m (h d) -> p m h d", d=P)
            v.wait_ge(*v.at(*net.proj_names(st["mkv"]), ("loaded", ("mem_gain", l, 1))))
            self.heads_vector(v, ("memk", l), x4(net.v_tok[:, :, 0:512]), self.sk_tok, [(0, 4, self.mem_gain[:, 1, :])],
                              done=("heads_normed", ("mem_k", l)))
            net.turn_copy(v, self.small_turn(("mem_k", l), net.v_tok, net.kT))
            self.rms_vector(v, ("memx", l), net.x, net.ax, 1)
            net.turn_copy(v, self.norm_turn(("memx", l), net.ax, net.xT))
            v.wait_ge(*v.at(*net.proj_names(st["mq"])))
            self.heads_vector(v, ("memq", l), x4(self.q_tok), self.sq_tok, [(0, 4, self.mem_gain[:, 0, :])], at=8,
                              done=("heads_normed", ("mem_q", l)))
            net.turn_copy(v, self.small_turn(("mem_q", l), self.q_tok, net.qT))
            attn_vector(net, v, f"mems{l}", self.mem_heads(), 2)
            ahead = (["router"] if l else []) + st["ffn"]["gate_up"][0]
            net.split_vector(v, ahead[:2])
            self.add_vector(v, n + 1, lambda m: [(st["mo"]["tag"], "full", b, m) for b in range(2)])
            self.rms_vector(v, ("ffn", l), net.x, net.ax, 3)
            net.turn_copy(v, self.norm_turn(("ffn", l), net.ax, net.xT_halves))
            net.split_vector(v, ahead[2:])
            if l:
                self.router_vector(v)
                ffn_vector(net, v, st["ffn"], lambda c, m: self.gates[:, m, self.each[c][0]:self.each[c][0] + 1])
            else:
                ffn_vector(net, v, st["ffn"])
            tag = st["ffn"]["tag"]
            self.add_vector(v, n + 2, lambda m: [(tag, "y", m, nb) for nb in range(2)])

    def gpsimd(self, pool):
        for l in range(2):
            if l == 0:
                pool.wait_ge(*pool.at(("loaded", ("const", 0))))
            rstd = lambda tag, at, n: self.net.rstd_gpsimd(pool, tag, self.hs[:, at:at + n], self.hr[:, at:at + n])
            self.rms_gpsimd(pool, ("mix", l))
            rstd(("dsa", l), 0, 18)
            rstd(("dsai", l), 20, 2)
            rstd(("kk", l), 0, 16)
            self.zeros_gpsimd(pool, l)
            rstd(("lnx", l), 16, 16)
            self.rms_gpsimd(pool, ("memt", l))
            rstd(("memk", l), 0, 8)
            self.rms_gpsimd(pool, ("memx", l))
            rstd(("memq", l), 8, 8)
            self.rms_gpsimd(pool, ("ffn", l))

PARTS = ("first", "second")


def _program(nc, ins, out, known, parts):
    with ExitStack() as ctx:
        net = Net(nc, ctx, ins, out, known)
        stages = []
        n = 0
        if "first" in parts:
            stages.append(First(net))
            n = 8
        else:
            net.load_param(("x", 0), net.x, ins["x"].rearrange("b (m p) n -> p (b m) n", p=P))
            net.load_param(("const", 0), net.consts[:, :], ins["constants"])
        if "second" in parts:
            stages.append(Second(net, n))
            n += 6
        block = ctx.enter_context(nc.Block())

        @block.sync
        def _(sp):
            e = Engine(net.led, sp, "sync")
            net.stream_sync(e)
            for m in range(MT):
                e.wait_ge(*e.at(("x", n, m)))
                sp.dma_start(out[0, m * P:(m + 1) * P, :], net.x[:, m, :]).then_inc(*e.mark("stored", ("stored", m), by=16))
            e.wait_ge(*e.at(("stored", 0), ("stored", 1)))

        @block.tensor
        def _(pe):
            e = Engine(net.led, pe, "tensor")
            for s in stages:
                s.tensor(e)

        @block.scalar
        def _(act):
            e = Engine(net.led, act, "scalar")
            for s in stages:
                s.scalar(e)

        @block.vector
        def _(v):
            e = Engine(net.led, v, "vector")
            for s in stages:
                s.vector(e)

        @block.gpsimd
        def _(pool):
            e = Engine(net.led, pool, "gpsimd")
            for s in stages:
                s.gpsimd(e)
        return net.led.values()



def kernel(**inputs):
    import concourse.bacc as bacc
    from concourse.bass_utils import run_bass_kernel_spmd

    arrays = {f"in_{name}": np.ascontiguousarray(a) for name, a in inputs.items()}
    arrays["in_constants"] = CONST_ARRAY

    def build(known):
        nc = bacc.Bacc("TRN2", target_bir_lowering=False, num_devices=1)
        ins = {name[3:]: nc.dram_tensor(name, a.shape, mybir.dt.from_np(a.dtype), kind="ExternalInput").ap()
               for name, a in arrays.items()}
        out = nc.dram_tensor("out", (1, S, D), F32, kind="ExternalOutput").ap()
        return nc, _program(nc, ins, out, known, PARTS)

    _, values = build(None)
    nc, _ = build(values)
    r = run_bass_kernel_spmd(nc, [arrays], core_ids=[0])
    return r.results[0]["out"]
```
